# Optimizing a Trainium2 kernel written in Bass

```python
import jax
import jax.numpy as jnp
from jax import lax
import numpy as np

D_MODEL = 1024
BATCH = 1
SEQ = 512
DEPTH = 1

CTX_LEN = 256
GRID_W = 64

RET_HEADS = 8
RET_DK = 64
RET_DV = 64
QK_WIDTH = RET_HEADS * RET_DK
RET_WIDTH = RET_HEADS * RET_DV
RET_CHUNK = 128
ROPE_PAIRS_PER_AXIS = RET_DK // 4
ROPE_BASE = 10000.0

FNET_GROUPS = 4
FNET_GROUP_DIM = 128
FNET_WIDTH = FNET_GROUPS * FNET_GROUP_DIM

MIX_WIDTH = RET_WIDTH + FNET_WIDTH

Q_OFF = 0
K_OFF = Q_OFF + QK_WIDTH
V_OFF = K_OFF + QK_WIDTH
G_OFF = V_OFF + RET_WIDTH
F_OFF = G_OFF + RET_WIDTH
IN_WIDTH = F_OFF + FNET_WIDTH

PEER_HEADS = 8
PEER_D_KEY = 256
PEER_N_KEYS = 128
PEER_N_EXPERTS = PEER_N_KEYS * PEER_N_KEYS
PEER_TOPK = 16
PEER_BLOCK = 128

N_MOD = 6
EPS = 1e-6

kernel_name = 'hybrid_retention_fnet_peer_dit_layer'

def _rms(x, gain):
    xf = x.astype(jnp.float32)
    y = xf * lax.rsqrt(jnp.mean(xf * xf, axis=-1, keepdims=True) + EPS)
    return (y * gain.astype(jnp.float32)).astype(x.dtype)

def _modulate(h, shift, scale):
    return h * (1 + scale) + shift

def _heads(t, d):
    b, n, _ = t.shape
    return t.reshape(b, n, -1, d).astype(jnp.float32)

def _axial_rope(rows):
    row_ids = jnp.repeat(jnp.arange(rows, dtype=jnp.float32), GRID_W)
    col_ids = jnp.tile(jnp.arange(GRID_W, dtype=jnp.float32), rows)
    freqs = ROPE_BASE ** (-jnp.arange(ROPE_PAIRS_PER_AXIS, dtype=jnp.float32) / ROPE_PAIRS_PER_AXIS)
    ang = jnp.concatenate([row_ids[:, None] * freqs[None, :], col_ids[:, None] * freqs[None, :]], axis=-1)
    return jnp.cos(ang), jnp.sin(ang)

def _rotate(t, cos, sin):
    half = t.shape[-1] // 2
    t1, t2 = t[..., :half], t[..., half:]
    cs = cos[None, :, None, :]
    sn = sin[None, :, None, :]
    return jnp.concatenate([t1 * cs - t2 * sn, t2 * cs + t1 * sn], axis=-1)

def _log_gamma(a):
    return jnp.log1p(-jnp.exp(a.astype(jnp.float32)))

def _retention_chunked(q, k, v, log_gamma, state0, strict):
    b, n, h, _ = q.shape
    c = RET_CHUNK
    nc = n // c

    def to_chunks(t):
        return t.reshape(b, nc, c, h, t.shape[-1]).transpose(1, 0, 3, 2, 4)

    qc, kc, vc = to_chunks(q), to_chunks(k), to_chunks(v)
    pos = jnp.arange(c, dtype=jnp.float32)
    diff = pos[:, None] - pos[None, :]
    allowed = diff > 0 if strict else diff >= 0
    decay_mask = jnp.where(allowed[None], jnp.exp(log_gamma[:, None, None] * jnp.maximum(diff, 0.0)[None]), 0.0)
    q_decay = jnp.exp(log_gamma[:, None] * (pos + 1.0)[None, :])
    k_decay = jnp.exp(log_gamma[:, None] * (c - 1.0 - pos)[None, :])
    chunk_decay = jnp.exp(log_gamma * c)

    def step(state, inp):
        qi, ki, vi = inp
        scores = jnp.einsum('bhid,bhjd->bhij', qi, ki) * decay_mask[None]
        inner = jnp.einsum('bhij,bhjv->bhiv', scores, vi)
        cross = jnp.einsum('bhid,bhdv->bhiv', qi, state) * q_decay[None, :, :, None]
        new_state = state * chunk_decay[None, :, None, None] + jnp.einsum('bhjd,bhjv->bhdv', ki * k_decay[None, :, :, None], vi)
        return new_state, inner + cross

    final, out = lax.scan(step, state0, (qc, kc, vc))
    out = out.transpose(1, 0, 3, 2, 4).reshape(b, n, h, v.shape[-1])
    return out, final

def _bidir_retention(q, k, v, log_gf, log_gb, state_f0, state_b0):
    out_f, st_f = _retention_chunked(q, k, v, log_gf, state_f0, False)
    flip = lambda t: jnp.flip(t, axis=1)
    out_b, st_b = _retention_chunked(flip(q), flip(k), flip(v), log_gb, state_b0, True)
    return out_f + flip(out_b), st_f, st_b

def _context_states(k, v, log_gf, log_gb):
    n = k.shape[1]
    pos = jnp.arange(n, dtype=jnp.float32)
    wf = jnp.exp(log_gf[:, None] * (n - 1.0 - pos)[None, :])
    wb = jnp.exp(log_gb[:, None] * pos[None, :])
    st_f = jnp.einsum('bnhd,hn,bnhv->bhdv', k, wf, v)
    st_b = jnp.einsum('bnhd,hn,bnhv->bhdv', k, wb, v)
    return st_f, st_b

def _fourier_mix(f):
    b, n, _ = f.shape
    fg = f.astype(jnp.float32).reshape(b, n, FNET_GROUPS, FNET_GROUP_DIM)
    return jnp.fft.fftn(fg, axes=(1, 3), norm='ortho').real.reshape(b, n, FNET_WIDTH)

def _mixer(h, w_in_l, log_gf, log_gb, ret_gain, state_f0, state_b0, rope):
    b, n, _ = h.shape
    proj = h @ w_in_l
    q = _heads(proj[..., Q_OFF:K_OFF], RET_DK)
    k = _heads(proj[..., K_OFF:V_OFF], RET_DK) * (RET_DK ** -0.5)
    v = _heads(proj[..., V_OFF:G_OFF], RET_DV)
    gate = proj[..., G_OFF:F_OFF].astype(jnp.float32)
    if rope is not None:
        cos, sin = rope
        q = _rotate(q, cos, sin)
        k = _rotate(k, cos, sin)
    ret, st_f, st_b = _bidir_retention(q, k, v, log_gf, log_gb, state_f0, state_b0)
    ret = ret * lax.rsqrt(jnp.mean(ret * ret, axis=-1, keepdims=True) + EPS)
    ret = ret.reshape(b, n, RET_WIDTH) * ret_gain.astype(jnp.float32) * jax.nn.silu(gate)
    four = _fourier_mix(proj[..., F_OFF:])
    mix = jnp.concatenate([ret, four], axis=-1).astype(h.dtype)
    return mix, st_f, st_b

def _peer(h, w_q, keys1, keys2, u, v):
    b, n, d = h.shape
    q = (h @ w_q).reshape(b, n, PEER_HEADS, PEER_D_KEY).astype(jnp.float32)
    half = PEER_D_KEY // 2
    s1 = jnp.einsum('bnhd,kd->bnhk', q[..., :half], keys1.astype(jnp.float32))
    s2 = jnp.einsum('bnhd,kd->bnhk', q[..., half:], keys2.astype(jnp.float32))
    v1, i1 = lax.top_k(s1, PEER_TOPK)
    v2, i2 = lax.top_k(s2, PEER_TOPK)
    cand = (v1[..., :, None] + v2[..., None, :]).reshape(b, n, PEER_HEADS, PEER_TOPK * PEER_TOPK)
    top_v, top_i = lax.top_k(cand, PEER_TOPK)
    e1 = jnp.take_along_axis(i1, top_i // PEER_TOPK, axis=-1)
    e2 = jnp.take_along_axis(i2, top_i % PEER_TOPK, axis=-1)
    ids = e1 * PEER_N_KEYS + e2
    wts = jax.nn.softmax(top_v, axis=-1)
    t = b * n
    nb = t // PEER_BLOCK
    k_all = PEER_HEADS * PEER_TOPK
    hb = h.reshape(nb, PEER_BLOCK, d)
    idb = ids.reshape(nb, PEER_BLOCK, k_all)
    wb = wts.reshape(nb, PEER_BLOCK, k_all)

    def block(args):
        hx, idx, w = args
        ue = jnp.take(u, idx, axis=0)
        act = jnp.einsum('td,tkd->tk', hx, ue).astype(jnp.float32)
        coef = (w * jax.nn.gelu(act, approximate=False)).astype(h.dtype)
        ve = jnp.take(v, idx, axis=0)
        return jnp.einsum('tk,tkd->td', coef, ve)

    out = lax.map(block, (hb, idb, wb))
    return out.reshape(b, n, d).astype(h.dtype)

def setup_inputs(seed: int = 0) -> dict:
    key = jax.random.key(seed)
    ks = jax.random.split(key, 24)
    f32 = jnp.float32

    def nrm(k, shape, scale):
        return jax.random.normal(k, shape, f32) * scale

    def gain(k, shape):
        return 1.0 + 0.05 * jax.random.normal(k, shape, f32)

    base_decay = -(5.0 + jnp.arange(RET_HEADS, dtype=f32)) * np.float32(np.log(2.0))
    return {
        'x': nrm(ks[0], (BATCH, SEQ, D_MODEL), 1.0),
        'c': nrm(ks[1], (BATCH, D_MODEL), 1.0),
        'ctx': nrm(ks[2], (BATCH, CTX_LEN, D_MODEL), 1.0),
        'c_ctx': nrm(ks[3], (D_MODEL,), 1.0),
        'w_ada': nrm(ks[4], (DEPTH, D_MODEL, N_MOD * D_MODEL), 0.5 * D_MODEL ** -0.5),
        'b_ada': nrm(ks[5], (DEPTH, N_MOD * D_MODEL), 0.01),
        'norm_pre_mix': gain(ks[6], (DEPTH, D_MODEL)),
        'norm_post_mix': gain(ks[7], (DEPTH, D_MODEL)),
        'w_in': nrm(ks[8], (DEPTH, D_MODEL, IN_WIDTH), D_MODEL ** -0.5),
        'ret_decay_fwd': base_decay[None, :] + nrm(ks[9], (DEPTH, RET_HEADS), 0.05),
        'ret_decay_bwd': base_decay[None, :] + nrm(ks[10], (DEPTH, RET_HEADS), 0.05),
        'ret_norm_gain': gain(ks[11], (DEPTH, RET_WIDTH)),
        'w_out': nrm(ks[12], (DEPTH, MIX_WIDTH, D_MODEL), MIX_WIDTH ** -0.5),
        'norm_pre_ffn': gain(ks[13], (DEPTH, D_MODEL)),
        'norm_post_ffn': gain(ks[14], (DEPTH, D_MODEL)),
        'peer_w_query': nrm(ks[15], (DEPTH, D_MODEL, PEER_HEADS * PEER_D_KEY), D_MODEL ** -0.5),
        'peer_sub_keys_1': nrm(ks[16], (DEPTH, PEER_N_KEYS, PEER_D_KEY // 2), (PEER_D_KEY // 2) ** -0.5),
        'peer_sub_keys_2': nrm(ks[17], (DEPTH, PEER_N_KEYS, PEER_D_KEY // 2), (PEER_D_KEY // 2) ** -0.5),
        'peer_u': nrm(ks[18], (DEPTH, PEER_N_EXPERTS, D_MODEL), D_MODEL ** -0.5),
        'peer_v': nrm(ks[19], (DEPTH, PEER_N_EXPERTS, D_MODEL), D_MODEL ** -0.5),
    }

def reference(x, c, ctx, c_ctx, w_ada, b_ada, norm_pre_mix, norm_post_mix, w_in, ret_decay_fwd, ret_decay_bwd, ret_norm_gain, w_out, norm_pre_ffn, norm_post_ffn, peer_w_query, peer_sub_keys_1, peer_sub_keys_2, peer_u, peer_v):
    n = x.shape[1]
    rows = n // GRID_W
    rope = _axial_rope(rows)
    for i in range(DEPTH):
        mod_x = (jax.nn.silu(c) @ w_ada[i] + b_ada[i])[:, None, :]
        mod_c = (jax.nn.silu(c_ctx) @ w_ada[i] + b_ada[i])[None, None, :]
        sh1, sc1, g1, sh2, sc2, g2 = jnp.split(mod_x, N_MOD, axis=-1)
        csh1, csc1, cg1, csh2, csc2, cg2 = jnp.split(mod_c, N_MOD, axis=-1)
        log_gf = _log_gamma(ret_decay_fwd[i])
        log_gb = _log_gamma(ret_decay_bwd[i])
        update_ctx = i + 1 < DEPTH

        hc = _modulate(_rms(ctx, norm_pre_mix[i]), csh1, csc1)
        if update_ctx:
            zeros = jnp.zeros((ctx.shape[0], RET_HEADS, RET_DK, RET_DV), jnp.float32)
            mix_c, st_f, st_b = _mixer(hc, w_in[i], log_gf, log_gb, ret_norm_gain[i], zeros, zeros, None)
        else:
            kv = hc @ w_in[i][:, K_OFF:G_OFF]
            k_c = _heads(kv[..., :QK_WIDTH], RET_DK) * (RET_DK ** -0.5)
            v_c = _heads(kv[..., QK_WIDTH:], RET_DV)
            st_f, st_b = _context_states(k_c, v_c, log_gf, log_gb)

        hx = _modulate(_rms(x, norm_pre_mix[i]), sh1, sc1)
        mix_x, _, _ = _mixer(hx, w_in[i], log_gf, log_gb, ret_norm_gain[i], st_f, st_b, rope)
        x = x + g1 * _rms(mix_x @ w_out[i], norm_post_mix[i])

        h2 = _modulate(_rms(x, norm_pre_ffn[i]), sh2, sc2)
        x = x + g2 * _rms(_peer(h2, peer_w_query[i], peer_sub_keys_1[i], peer_sub_keys_2[i], peer_u[i], peer_v[i]), norm_post_ffn[i])

        if update_ctx:
            ctx = ctx + cg1 * _rms(mix_c @ w_out[i], norm_post_mix[i])
            hc2 = _modulate(_rms(ctx, norm_pre_ffn[i]), csh2, csc2)
            ctx = ctx + cg2 * _rms(_peer(hc2, peer_w_query[i], peer_sub_keys_1[i], peer_sub_keys_2[i], peer_u[i], peer_v[i]), norm_post_ffn[i])
    return x


_drawn_inputs = setup_inputs


def setup_inputs(seed=0):
    import zlib

    import numpy as np

    out = dict(_drawn_inputs(seed))
    spreads = {}
    factors = {'norm_post_ffn': 3.984}
    for name, (base, spread) in spreads.items():
        noise = np.random.default_rng([zlib.crc32(name.encode()), seed]).standard_normal(out[name].shape)
        drawn = base * np.exp(spread * noise) if base else spread * noise
        out[name] = jnp.asarray(drawn.astype(out[name].dtype))
    for name, factor in factors.items():
        out[name] = (out[name] * factor).astype(out[name].dtype)
    return out
```

```python
from contextlib import ExitStack

import numpy as np

import concourse.bass as bass
from concourse import mybir

F32 = mybir.dt.float32
F32R = mybir.dt.float32r
U32 = mybir.dt.uint32
ALU = mybir.AluOpType
ACT = mybir.ActivationFunctionType
AX = mybir.AxisListType.X

P = 128
D = 1024
KC = D // P
N = 512
TB = N // P
NCTX = 256
CB = NCTX // P
GRID_W = 64
HEADS = 8
DH = 64
PAIRS = HEADS // 2
W512 = 512
GROUPS = 4
EPS = 1e-6
PH = 8
TOPK = 16
PICKS = PH * TOPK
KEYS = 128
EB = 128
MASKW = N + N - P
NEG = -3.0e38

RAW = 4
SPLIT = 4
PART_A = 48
TOK_STEP = 8
PART_B = N // TOK_STEP
GRP = 8

C_C, C_BADA, C_NPM, C_NPF, C_DECP, C_DECH, C_END = 0, 16, 64, 72, 80, 88, 104
ROPE_KINDS = 6


def plan_units():
    units = [("ada", c * P, 0) for c in range(2 * KC)]
    for piece in (1, 2, 4, 0, 3):
        units += [("in", piece * W512, j) for j in range(4)]
    units += [("ada", 2 * D + c * P, 0) for c in range(KC)]
    units += [("ada", 5 * D + c * P, 0) for c in range(KC)]
    units += [("ada", 3 * D + c * P, 0) for c in range(2 * KC)]
    for half in range(2):
        units += [("out", half * W512, j) for j in range(4)]
    units += [("q", c * P, 0) for c in range(2 * PH)]
    return units


def build(nc, x, ctxt, cols, w_ada, rows, w_in, w_out, w_q, keys, u_t, v_nat, rope, dft, dft_small, ident_in,
          out, g_dram, w_dram):
    units = plan_units()
    first_of = {}
    ada_index, split_index = {}, {}
    for n, (kind, _, _) in enumerate(units):
        first_of.setdefault(kind, n)
        if kind == "ada":
            ada_index[n] = len(ada_index)
        else:
            split_index[n] = len(split_index)
    split_units = [n for n in range(len(units)) if n in split_index]
    n_split = len(split_units)

    es = ExitStack()
    with es:
        def sem(name):
            return es.enter_context(nc.semaphore(name))

        base = 16896
        K = 1024
        rA = base
        rC = rA + 32 * K
        rH = rC + 16 * K
        rD = rH + 8 * K
        rE = rD + 16 * K
        rJ = rE + 32 * K
        rF = rJ + 16 * K
        rG = rF + 16 * K
        rB = rG + 16 * K
        rI = rB + 16 * K
        rS = rI + 16 * K
        small_at = [rS]

        def at(name, offset, shape, dt=F32):
            return nc.alloc_sbuf_tensor_at(name, [P] + shape, dt, offset=offset)

        def small(name, shape, dt=F32):
            size = 4 * int(np.prod(shape))
            t = at(name, small_at[0], shape, dt)
            small_at[0] += -(-size // 64) * 64
            assert small_at[0] <= 229344
            return t

        hT_hi = at("hT_hi", rA, [KC, N], F32R)
        hT_lo = at("hT_lo", rA + 16 * K, [KC, N], F32R)
        dft_hi = at("dft_hi", rA, [2 * TB, N], F32R)
        dft_lo = at("dft_lo", rA + 16 * K, [2 * TB, N], F32R)
        mask = at("mask", rA, [2, MASKW])
        q_dec = at("q_dec", rA + 7 * K, [2, 2, N])
        ck_w = at("ck_w", rA + 15 * K, [2, CB, W512])
        pos_rows = at("pos_rows", rA + 23 * K, [2, N])
        dec_rows = at("dec_rows", rA + 27 * K, [2, N])
        xs = at("xs", rC, [TB, D])
        dft_raw = at("dft_raw", rC, [2 * TB, N])
        x2 = at("x2", rC, [TB, D])
        gate = at("gate", rH, [TB, W512])
        gg = at("gg", rH, [2, D])
        raw = at("raw", rD, [RAW, D])
        blk_raw = at("blk_raw", rD, [2, D])
        g_buf = at("g_buf", rD + 8 * K, [2, N])
        ws_hi = [at(f"ws_hi{i}", rE + 8 * K * i, [D], F32R) for i in range(SPLIT)]
        ws_lo = [at(f"ws_lo{i}", rE + 8 * K * i + 4 * K, [D], F32R) for i in range(SPLIT)]
        y_hi = at("y_hi", rE, [2, 2, N], F32R)
        y_lo = at("y_lo", rE + 8 * K, [2, 2, N], F32R)
        scores = at("scores", rE, [4, TB, N])
        picks = at("picks", rE + 16 * K, [3, TB, PICKS])
        onehot = at("onehot", rE + 16 * K, [2, 3, TOK_STEP, P], F32R)
        rope_tmp = at("rope_tmp", rJ, [2, 2, W512])
        cx = at("cx", rJ + 8 * K, [CB, D])
        four_hi = at("four_hi", rJ, [GROUPS, N], F32R)
        four_lo = at("four_lo", rJ + 8 * K, [GROUPS, N], F32R)
        q_t = at("q_t", rJ, [2, N])
        picks_t = at("picks_t", rJ + 8 * K, [4, N])
        coef = at("coef", rE + 16 * K, [2, N])
        coef_hi = at("coef_hi", rE + 20 * K, [2, N], F32R)
        coef_lo = at("coef_lo", rE + 24 * K, [2, N], F32R)
        q_sb = at("q_sb", rF, [TB, W512])
        k_sb = at("k_sb", rF + 8 * K, [TB, W512])
        v_sb = at("v_sb", rG, [TB, W512])
        cv_sb = at("cv_sb", rG + 8 * K, [CB, W512])
        ck_sb = at("ck_sb", rG + 12 * K, [CB, W512])
        cT_hi = at("cT_hi", rB, [KC, NCTX], F32R)
        cT_lo = at("cT_lo", rB + 8 * K, [KC, NCTX], F32R)
        qT = at("qT", rB, [PAIRS, N])
        kT = at("kT", rB + 8 * K, [PAIRS, N])
        f_hi = at("f_hi", rI, [TB, W512], F32R)
        f_lo = at("f_lo", rI + 8 * K, [TB, W512], F32R)
        ret_hi = at("ret_hi", rI, [PAIRS, N], F32R)
        ret_lo = at("ret_lo", rI + 8 * K, [PAIRS, N], F32R)
        delta = at("delta", rF, [MASKW])
        r_fwd = at("r_fwd", rF + 3584, [MASKW])
        r_bwd = at("r_bwd", rF + 7168, [MASKW])
        expo = at("expo", rF + 10752, [MASKW])
        ret_tmp = at("ret_tmp", rF, [2, W512])
        mix_r = at("mix_r", rF + 4 * K, [TB, W512])
        row_in = at("row_in", rG, [4, D])
        xn2 = at("xn2", rG, [TB, D])
        out_tmp = at("out_tmp", rF, [2, 512])
        s_all = at("s_all", rF, [TB, 2 * PH * KEYS])
        s_work = at("s_work", rB, [2, PH, KEYS])
        cand = at("cand", rB + 8 * K, [PH, TOPK, TOPK])
        eq = at("eq", rI, [PH, TOPK, TOPK])
        w_stage = at("w_stage", rF, [2, EB, 64])
        grp_g = at("grp_g", rF, [2, GRP, N])
        grp_w = at("grp_w", rF + 32 * K, [2, N // 64, GRP, 64])
        fin = at("fin", rF, [TB, D])
        colp = small("colp", [C_END])
        ident = small("ident", [P])
        rope_sb = small("rope_sb", [TB, ROPE_KINDS, 32])
        csil = small("csil", [KC, 2])
        ret_gain = small("ret_gain", [W512])
        keys_sb = small("keys_sb", [2, KEYS])
        dfs_raw = small("dfs_raw", [2, P])
        dfs_hi = small("dfs_hi", [2, P], F32R)
        dfs_lo = small("dfs_lo", [2, P], F32R)
        mod_a = small("mod_a", [KC, 2])
        mod_b = small("mod_b", [KC, 2])
        mod_t = small("mod_t", [KC, 2])
        ss = small("ss", [8])
        rs = small("rs", [8])
        ss_ret = small("ss_ret", [TB, HEADS])
        rs_ret = small("rs_ret", [TB, HEADS])
        lg = small("lg", [24])
        lgt = small("lgt", [6, 24])
        ck_pos = small("ck_pos", [2, CB])
        ck_dec = small("ck_dec", [2, CB, HEADS])
        s_diag = small("s_diag", [2, PAIRS, P])
        iota_e = small("iota_e", [P])
        iota_k = small("iota_k", [TOPK])
        c_rows_at = small_at[0]
        c_rows = small("c_rows", [KC, P])
        tv = at("tv", c_rows_at, [2, PH, TOPK])
        ti = at("ti", c_rows_at + K, [2, PH, TOPK], U32)
        tif = at("tif", c_rows_at + 2 * K, [2, PH, TOPK])
        cpf = at("cpf", c_rows_at + 3 * K, [2, PICKS])
        cur = small("cur", [2, 4, TOK_STEP])
        cp = small("cp", [PICKS], U32)
        cpa = small("cpa", [2, PICKS], U32)
        sm = small("sm", [TB * PH])
        guard = small("guard", [1])
        full = at("full", rJ, [2, N])
        junk = at("junk", rJ + 4 * K, [D])
        full2 = at("full2", rI, [2, N])
        junk2 = at("junk2", rF + 12 * K, [D])

        ps = es.enter_context(nc.psum_tensor("ps", [P, 8, 512], F32))

        cols_in, ident_ld, x_in, cx_in = sem("cols_in"), sem("ident_ld"), sem("x_in"), sem("cx_in")
        rope_in, tail_in, dft_in, rows_in, x_again = (
            sem("rope_in"), sem("tail_in"), sem("dft_in"), sem("rows_in"), sem("x_again"))
        gain_in = sem("gain_in")
        raw_in = [sem(f"raw_in{i}") for i in range(RAW)]
        ada_used, split_hi, split_lo, split_used = (
            sem("ada_used"), sem("split_hi"), sem("split_lo"), sem("split_used"))
        iotas, silu_done, crow_done, lg_step = sem("iotas"), sem("silu_done"), sem("crow_done"), sem("lg_step")
        lg_act = sem("lg_act")
        mod_step = sem("mod_step")
        sq_done, ms_done, rt_done, rs_done = sem("sq_done"), sem("ms_done"), sem("rt_done"), sem("rs_done")
        xn_done = sem("xn_done")
        tr_done, full_done, full_hi, full_lo = sem("tr_done"), sem("full_done"), sem("full_hi"), sem("full_lo")
        proj_taken, f_rest, rope_step, gate_done = (
            sem("proj_taken"), sem("f_rest"), sem("rope_step"), sem("gate_done"))
        dft_r, dft_l = sem("dft_r"), sem("dft_l")
        qk_tr, qk_taken = sem("qk_tr"), sem("qk_taken")
        dft1_done, y_r, y_l, dft2_done, four_r, four_l = (
            sem("dft1_done"), sem("y_r"), sem("y_l"), sem("dft2_done"), sem("four_r"), sem("four_l"))
        ret_step, ret_act, st_done, st_taken = sem("ret_step"), sem("ret_act"), sem("st_done"), sem("st_taken")
        ckd_done, ckw_done = sem("ckd_done"), sem("ckw_done")
        expo_done, mask_done, sc_done, msc_done, ret_done = (
            sem("expo_done"), sem("mask_done"), sem("sc_done"), sem("msc_done"), sem("ret_done"))
        dec_done, qd_done = sem("dec_done"), sem("qd_done")
        rsq_done, rss_done, rrt_done, nrm_step, mixr_done = (
            sem("rsq_done"), sem("rss_done"), sem("rrt_done"), sem("nrm_step"), sem("mixr_done"))
        mtr_done, ret_r, ret_l = sem("mtr_done"), sem("ret_r"), sem("ret_l")
        gg_step, x2_step = sem("gg_step"), sem("x2_step")
        y_scaled = sem("y_scaled")
        q_taken, s_done, s_taken = sem("q_taken"), sem("s_done"), sem("s_taken")
        top_step, exp_done, soft_step = (
            sem("top_step"), sem("exp_done"), sem("soft_step"))
        ptr_done, ptr_taken = sem("ptr_done"), sem("ptr_taken")
        blk_in = [sem("blk_in0"), sem("blk_in1")]
        u_hi, u_lo, act_done, gelu_done = sem("u_hi"), sem("u_lo"), sem("act_done"), sem("gelu_done")
        g_out = [sem("g_out0"), sem("g_out1")]
        cur_done, oh_done, w_mm, w_evac = sem("cur_done"), sem("oh_done"), sem("w_mm"), sem("w_evac")
        w_stored = [sem("w_stored0"), sem("w_stored1")]
        v_in = [sem("v_in0"), sem("v_in1")]
        v_hi, v_lo, coef_done, coef_r, coef_l, v_mm = (
            sem("v_hi"), sem("v_lo"), sem("coef_done"), sem("coef_r"), sem("coef_l"), sem("v_mm"))
        grp_in = [sem("grp_in0"), sem("grp_in1")]
        group_seen = sem("group_seen")
        fsq_done, fin_act, fin_step, out_done = sem("fsq_done"), sem("fin_act"), sem("fin_step"), sem("out_done")

        dram_k = {"ada": w_ada, "in": w_in, "out": w_out, "q": w_q}

        def unit_src(n):
            kind, c0, j = units[n]
            src = dram_k[kind].rearrange("(c p) n -> p c n", p=P)
            if kind in ("ada", "q"):
                return src[:, :, c0:c0 + P]
            return src[:, 2 * j:2 * j + 2, c0:c0 + W512]

        def unit_dst(n):
            t = raw[:, n % RAW, :]
            return t.rearrange("p (c n) -> p c n", c=KC if units[n][0] in ("ada", "q") else 2)

        def raw_ready(eng, n):
            eng.wait_ge(raw_in[n % RAW], 16 * (n // RAW + 1))

        n_proj = 5
        x_banks = [[0, 1, 2, 3], [6, 7, 0, 1], [4, 5, 6, 7], [0, 1, 2, 3], [4, 5, 6, 7]]
        c_banks = [[4, 5], [2, 3], [], [], []]
        bank_free = [[0] * 6, [0, 0, 1, 2, 3, 4], [6, 6, 7, 8], [9, 10, 11, 12], [0, 0, 0, 0]]
        ada_rest = [n for n in range(len(units)) if units[n][0] == "ada"][2 * KC:]

        block = es.enter_context(nc.Block())

        @block.sync
        def _(sp):
            def load_unit(n):
                if n >= RAW:
                    m = n - RAW
                    if m in ada_index:
                        sp.wait_ge(ada_used, ada_index[m] + 1)
                    else:
                        sp.wait_ge(split_lo, split_index[m] + 1)
                sp.dma_start(unit_dst(n), unit_src(n)).then_inc(raw_in[n % RAW], 16)

            for n in range(len(units)):
                if n == first_of["in"] + 8:
                    sp.wait_ge(tr_done, 2 * KC)
                    sp.dma_start(dft_raw[:], dft).then_inc(dft_in, 16)
                if n == ada_rest[0] + 3:
                    sp.wait_ge(dft_l, 4)
                    sp.dma_start(x2[:], x.rearrange("(b p) d -> p b d", p=P)).then_inc(x_again, 16)
                if n == ada_rest[0] + 4:
                    sp.wait_ge(ret_done, PAIRS)
                    for r in range(4):
                        sp.dma_start(row_in[:, r, :], rows[r:r + 1, :].broadcast_to([P, D])).then_inc(rows_in, 16)
                load_unit(n)

            def load_u(b, p, free):
                if free is not None:
                    sp.wait_ge(u_lo, free)
                sp.dma_start(blk_raw[:, p, :], u_t[bass.ds(b, 1), :, :].rearrange("a p n -> p (a n)")).then_inc(blk_in[p], 16)

            def store_g(b, p):
                sp.wait_ge(gelu_done, b + 1)
                sp.dma_start(g_dram[:, bass.ds(b * N, N)], g_buf[:, p, :]).then_inc(g_out[p], 16)

            sp.wait_ge(split_lo, n_split)
            load_u(0, 0, None)
            load_u(1, 1, None)
            with sp.Fori(0, PART_A // 2) as i:
                for p in range(2):
                    load_u(2 * i + (p + 2), p, 2 * i + (p + 1))
                    store_g(2 * i + p, p)

            def store_w(g, half):
                sp.wait_ge(w_evac, 16 * g + 16)
                sp.dma_start(w_dram[bass.ds(g, 1), :, :].rearrange("a p n -> p (a n)"),
                             w_stage[:, half, :, :].rearrange("p b t -> p (b t)")).then_inc(w_stored[half], 16)

            with sp.Fori(0, PART_B // 16) as o:
                for half in range(2):
                    with sp.Fori(0, 4) as i:
                        for p in range(2):
                            b = 16 * o + 2 * i + (PART_A + 8 * half + p)
                            load_u(b + 2, p, b + 1)
                            store_g(b, p)
                    store_w(2 * o + half, half)

            def load_group(g, p, free):
                if free is not None:
                    sp.wait_ge(coef_done, free)
                sp.dma_start(grp_g[:, p, :, :].rearrange("p b t -> p (b t)"),
                             g_dram[:, bass.ds(g * (GRP * N), GRP * N)]).then_inc(grp_in[p], 16)
                sp.dma_start(grp_w[:, p, :, :, :].rearrange("p a b t -> p a (b t)"),
                             w_dram[:, :, bass.ds(g * (GRP * 64), GRP * 64)].rearrange("a p n -> p a n")).then_inc(grp_in[p], 16)

            def part_c(b, p):
                if isinstance(b, int) and b + 2 >= EB:
                    sp.wait_ge(u_lo, b + 1)
                    sp.dma_start(blk_raw[:, p, :], v_nat[(b + 2 - EB) * P:(b + 3 - EB) * P, :]).then_inc(v_in[p], 16)
                else:
                    load_u(b + 2, p, b + 1)
                store_g(b, p)

            c0 = PART_A + PART_B
            for p in range(2):
                part_c(c0 + p, p)
            for p in range(2):
                sp.wait_ge(w_stored[p], 16 * (PART_B // 16))
                sp.wait_ge(g_out[p], 16 * (c0 // 2))
            for g in range(2):
                load_group(g, g, None)
            with sp.Fori(c0 // 2 + 1, EB // 2 - 1) as i:
                for p in range(2):
                    part_c(2 * i + p, p)
            for p in range(2):
                part_c(EB - 2 + p, p)
            for p in range(2):
                sp.wait_ge(g_out[p], 16 * (EB // 2))

            def load_v(b, p):
                sp.wait_ge(v_lo, b + (-1))
                sp.dma_start(blk_raw[:, p, :], v_nat[bass.ds(b * P, P), :]).then_inc(v_in[p], 16)

            with sp.Fori(0, EB // GRP // 2 - 1) as o:
                for half in range(2):
                    with sp.Fori(0, GRP // 2) as i:
                        for p in range(2):
                            load_v(16 * o + 2 * i + (8 * half + p + 2), p)
                    load_group(2 * o + (half + 2), half, 16 * o + (8 * half + 8))
            with sp.Fori(0, GRP - 1) as i:
                for p in range(2):
                    load_v(2 * i + (EB - 16 + p + 2), p)

            for tb in range(TB):
                sp.wait_ge(fin_step, 2 * TB + 2 * (tb + 1))
                sp.dma_start(out.rearrange("(b p) d -> p b d", p=P)[:, tb, :], fin[:, tb, :]).then_inc(out_done, 16)
            sp.wait_ge(out_done, 16 * TB)

        @block.gpsimd
        def _(pool):
            pool.iota(iota_e[:], [[1, P]], base=0, channel_multiplier=0,
                      allow_small_or_imprecise_dtypes=True).then_inc(iotas, 1)
            pool.iota(iota_k[:], [[1, TOPK]], base=0, channel_multiplier=0,
                      allow_small_or_imprecise_dtypes=True).then_inc(iotas, 1)
            pool.iota(ck_pos[:, 0, :], [[-P, CB]], base=NCTX - 1, channel_multiplier=-1,
                      allow_small_or_imprecise_dtypes=True).then_inc(iotas, 1)
            pool.iota(ck_pos[:, 1, :], [[P, CB]], base=0, channel_multiplier=1,
                      allow_small_or_imprecise_dtypes=True).then_inc(iotas, 1)
            pool.memset(s_diag[:], 0.0).then_inc(iotas, 1)
            pool.wait_ge(qk_tr, 8)
            pool.iota(delta[:], [[1, MASKW]], base=-(N - P), channel_multiplier=-1,
                      allow_small_or_imprecise_dtypes=True).then_inc(iotas, 1)
            pool.wait_ge(dft1_done, 8)
            pool.iota(pos_rows[:, 0, :], [[1, N]], base=1, channel_multiplier=0,
                      allow_small_or_imprecise_dtypes=True).then_inc(iotas, 1)
            pool.iota(pos_rows[:, 1, :], [[-1, N]], base=N, channel_multiplier=0,
                      allow_small_or_imprecise_dtypes=True).then_inc(iotas, 1)

            def rest(b, p):
                pool.wait_ge(u_hi, b + 1)
                pool.tensor_tensor(ws_lo[p][:], blk_raw[:, p, :], ws_hi[p][:].bitcast(F32), ALU.subtract).then_inc(u_lo, 1)

            with pool.Fori(0, EB // 2) as i:
                for p in range(2):
                    rest(2 * i + p, p)

        @block.scalar
        def _(act):
            act.dma_start(colp[:], cols).then_inc(cols_in, 16)
            act.dma_start(xs[:], x.rearrange("(b p) d -> p b d", p=P)).then_inc(x_in, 16)
            act.dma_start(cx[:], ctxt.rearrange("(b p) d -> p b d", p=P)).then_inc(cx_in, 16)
            act.dma_start(ident[:], ident_in).then_inc(ident_ld, 16)
            act.dma_start(rope_sb[:], rope).then_inc(rope_in, 16)
            act.dma_start(ret_gain[:], rows[4:5, 0:W512].broadcast_to([P, W512])).then_inc(gain_in, 16)
            act.dma_start(dfs_raw[:], dft_small).then_inc(tail_in, 16)
            act.dma_start(keys_sb[:], keys).then_inc(tail_in, 16)

            act.wait_ge(cols_in, 16)
            act.activation(csil[:].rearrange("p c t -> p (c t)"), colp[:, C_C:C_BADA], ACT.Silu).then_inc(silu_done, 1)
            act.activation(lgt[:, 0, :], colp[:, C_DECP:C_END], ACT.Exp).then_inc(lg_act, 1)
            act.wait_ge(lg_step, 1)
            act.activation(lgt[:, 2, :], lgt[:, 1, :], ACT.Ln).then_inc(lg_act, 1)

            def squares(srcs, to, first):
                for m, (src, bank) in enumerate(srcs):
                    if first + m:
                        act.wait_ge(sq_done, first + m)
                    act.activation(junk[:] if to is None else to, src, ACT.Square,
                                   accum_out=ss[:, bank:bank + 1]).then_inc(sq_done, 1)

            act.wait_ge(x_in, 16)
            squares([(xs[:, tb, :], tb) for tb in range(TB)], None, 0)
            act.wait_ge(cx_in, 16)
            squares([(cx[:, tb, :], TB + tb) for tb in range(CB)], None, TB)
            act.wait_ge(ms_done, 1)
            act.activation(rs[:, 0:6], ss[:, 0:6], ACT.Sqrt).then_inc(rt_done, 1)

            def round_full(src, dst, m):
                act.wait_ge(full_done, m + 1)
                act.activation(dst, src, ACT.Copy).then_inc(full_hi, 1)

            for kc in range(KC):
                round_full(full[:, 0, :], hT_hi[:, kc, :], 2 * kc)
                round_full(full[:, 1, 0:NCTX], cT_hi[:, kc, :], 2 * kc + 1)

            def round_unit(n):
                s = split_index[n]
                raw_ready(act, n)
                if s >= SPLIT:
                    act.wait_ge(split_used, s - SPLIT + 1)
                act.activation(ws_hi[s % SPLIT][:], raw[:, n % RAW, :], ACT.Copy).then_inc(split_hi, 1)

            def take_piece(p):
                act.wait_ge(split_used, 4 * p + 4)
                for tb in range(TB):
                    src = ps[:, x_banks[p][tb], :]
                    dst, f = [(k_sb[:, tb, :], ACT.Copy), (v_sb[:, tb, :], ACT.Copy), (f_hi[:, tb, :], ACT.Copy),
                              (q_sb[:, tb, :], ACT.Copy), (gate[:, tb, :], ACT.Silu)][p]
                    act.activation(dst, src, f).then_inc(proj_taken, 1)
                for cb in range(CB if p < 2 else 0):
                    src = ps[:, c_banks[p][cb], :]
                    act.activation([ck_sb, cv_sb][p][:, cb, :], src, ACT.Copy,
                                   scale=[DH ** -0.5, 1.0][p]).then_inc(proj_taken, 1)

            for p in range(n_proj):
                for j in range(4):
                    round_unit(split_units[4 * p + j])
                if p:
                    take_piece(p - 1)
            take_piece(n_proj - 1)
            act.wait_ge(dft_in, 16)
            for m in range(4):
                act.activation(dft_hi[:, 2 * m:2 * m + 2, :], dft_raw[:, 2 * m:2 * m + 2, :], ACT.Copy).then_inc(dft_r, 1)
            act.wait_ge(tail_in, 32)
            act.activation(dfs_hi[:], dfs_raw[:], ACT.Copy).then_inc(dft_r, 1)
            for m in range(8):
                act.wait_ge(qk_tr, m + 1)
                act.activation((kT if m < 4 else qT)[:, m % 4, :], ps[:, m % 4, :], ACT.Copy).then_inc(qk_taken, 1)

            def round_y(g):
                for t in range(2):
                    act.wait_ge(dft1_done, 2 * g + t + 1)
                    if g >= 2:
                        act.wait_ge(dft2_done, g - 1)
                    act.activation(y_hi[:, g % 2, t, :], ps[:, 2 * g + t, :], ACT.Copy).then_inc(y_r, 1)

            def round_four(g):
                act.wait_ge(dft2_done, g + 1)
                act.activation(four_hi[:, g, :], ps[:, 2 * g, :], ACT.Copy).then_inc(four_r, 1)

            round_y(0)
            round_y(1)
            round_four(0)
            round_y(2)
            round_four(1)
            round_y(3)
            round_four(2)
            round_four(3)
            act.wait_ge(ckd_done, 4)
            act.activation(ck_dec[:], ck_dec[:], ACT.Exp).then_inc(ret_act, 1)

            def decays(c2):
                for d in range(2):
                    act.wait_ge(iotas, 8)
                    if 2 * c2 + d >= 2:
                        act.wait_ge(qd_done, 2 * c2 + d - 1)
                    act.activation(dec_rows[:, d, :], pos_rows[:, d, :], ACT.Exp,
                                   scale=lg[:, d * PAIRS + c2:d * PAIRS + c2 + 1]).then_inc(dec_done, 1)

            for c2 in range(PAIRS):
                decays(c2)
                for h in (2 * c2, 2 * c2 + 1):
                    act.wait_ge(expo_done, h + 1)
                    if h >= 2:
                        act.wait_ge(msc_done, 4 * (h - 1))
                    act.activation(mask[:, h % 2, :], expo[:], ACT.Exp).then_inc(mask_done, 1)
            for ib in range(TB):
                act.wait_ge(ret_done, PAIRS)
                if ib >= 2:
                    act.wait_ge(rss_done, ib - 1)
                act.activation(ret_tmp[:, ib % 2, :], ps[:, 4 + ib, :], ACT.Square).then_inc(rsq_done, 1)
            act.wait_ge(rss_done, TB + 1)
            act.activation(rs_ret[:], ss_ret[:], ACT.Sqrt).then_inc(rrt_done, 1)
            for c2 in range(PAIRS):
                act.wait_ge(mtr_done, c2 + 1)
                act.activation(ret_hi[:, c2, :], ps[:, c2, :], ACT.Copy).then_inc(ret_r, 1)
            for m in range(8):
                round_unit(split_units[20 + m])
            for half in range(2):
                act.wait_ge(split_used, 24 + 4 * half)
                for tb in range(TB):
                    m = 4 * half + tb
                    act.wait_ge(sq_done, 6 + m)
                    act.activation(junk2[:, 0:W512], ps[:, m, :], ACT.Square,
                                   accum_out=ss[:, m:m + 1]).then_inc(sq_done, 1)
            act.wait_ge(ms_done, 3)
            act.activation(rs[:, 0:4], ss[:, 0:4], ACT.Sqrt).then_inc(rt_done, 1)
            for tb in range(TB):
                act.wait_ge(x2_step, 2 * tb + 2)
                act.wait_ge(sq_done, 14 + tb)
                act.activation(junk2[:], x2[:, tb, :], ACT.Square, accum_out=ss[:, 4 + tb:5 + tb]).then_inc(sq_done, 1)
            act.wait_ge(ms_done, 4)
            act.activation(rs[:, 4:8], ss[:, 4:8], ACT.Sqrt).then_inc(rt_done, 1)
            for m in range(KC):
                round_full(full2[:, m % 2, :], hT_hi[:, m, :], 2 * KC + m)
            def take_q(m):
                act.wait_ge(split_used, 28 + m + 1)
                if m >= 2:
                    act.wait_ge(s_done, m - 1)
                act.activation(q_t[:, m % 2, :], ps[:, 6 + m % 2, :], ACT.Copy).then_inc(q_taken, 1)

            for m in range(2 * PH):
                round_unit(split_units[28 + m])
                if m >= 2:
                    take_q(m - 2)
            take_q(2 * PH - 2)
            take_q(2 * PH - 1)

            def round_u(b, p, used, used_value):
                act.wait_ge(blk_in[p], b * 8 + (16 - 8 * p))
                act.wait_ge(used, used_value)
                act.activation(ws_hi[p][:], blk_raw[:, p, :], ACT.Copy).then_inc(u_hi, 1)

            def gelu(b, p, first=False):
                act.wait_ge(act_done, b + 1)
                if not first:
                    act.wait_ge(g_out[p], b * 8 + (-8 * p))
                act.activation(g_buf[:, p, :], ps[:, p, :], ACT.Gelu).then_inc(gelu_done, 1)

            def take_w(q, p, half, t0):
                for r in range(2):
                    act.wait_ge(w_mm, q + 1)
                    dst = w_stage[:, half, :, bass.ds(t0 + 4 * r, 4)]
                    src = ps[:, 2 + 2 * p + r, :].rearrange("p (t b) -> p b t", t=4)
                    act.activation(dst, src, ACT.Copy).then_inc(w_evac, 1)

            round_u(0, 0, split_used, n_split - 3)
            round_u(1, 1, split_used, n_split - 2)
            gelu(0, 0, True)
            round_u(2, 0, act_done, 1)
            gelu(1, 1, True)
            with act.Fori(1, PART_A // 2) as i:
                for p in range(2):
                    b = 2 * i + p
                    round_u(b + 1, 1 - p, act_done, b)
                    gelu(b, p)
            act.wait_ge(top_step, TB * (1 + 10 * PH + 5 + 1 + 5 * PH + 5 + 4 + 1 + 2 * 3 + 1))
            act.activation(picks[:, 2, :, :], picks[:, 2, :, :], ACT.Exp).then_inc(exp_done, 1)
            act.wait_ge(ptr_taken, 3)
            act.activation(picks_t[:, 2, :].bitcast(F32R), picks_t[:, 3, :], ACT.Copy).then_inc(ptr_taken, 1)

            def part_b(o, half):
                with act.Fori(0, 4) as i:
                    for p in range(2):
                        q = 16 * o + 2 * i + (8 * half + p)
                        b = q + PART_A
                        round_u(b + 1, 1 - p, act_done, b)
                        gelu(b, p)
                        take_w(q, p, half, 16 * i + 8 * p)

            for half in range(2):
                part_b(0, half)
            with act.Fori(1, PART_B // 16) as o:
                for half in range(2):
                    act.wait_ge(w_stored[half], 16 * o)
                    part_b(o, half)
            with act.Fori((PART_A + PART_B) // 2, EB // 2 - 1) as i:
                for p in range(2):
                    b = 2 * i + p
                    round_u(b + 1, 1 - p, act_done, b)
                    gelu(b, p)
            round_u(EB - 1, 1, act_done, EB - 2)
            gelu(EB - 2, 0)
            gelu(EB - 1, 1)

            def round_v(b, p, used, used_value):
                act.wait_ge(v_in[p], b * 8 + (16 - 8 * p))
                act.wait_ge(used, used_value)
                act.activation(ws_hi[p][:], blk_raw[:, p, :], ACT.Copy).then_inc(v_hi, 1)
                act.wait_ge(coef_done, b + 1)
                act.activation(coef_hi[:, p, :], coef[:, p, :], ACT.Copy).then_inc(coef_r, 1)

            for b in range(2):
                round_v(b, b, act_done, EB - 1 + b)
            with act.Fori(1, EB // 2) as i:
                for p in range(2):
                    b = 2 * i + p
                    round_v(b, p, v_mm, b + (-1))
            for m in range(8):
                act.wait_ge(v_mm, EB)
                if m:
                    act.wait_ge(fsq_done, m)
                act.activation(full2[:, 0, :], ps[:, m, :], ACT.Square, accum_out=ss[:, m:m + 1]).then_inc(fsq_done, 1)
            act.wait_ge(fin_act, 1)
            act.activation(rs[:, 0:4], ss[:, 0:4], ACT.Sqrt).then_inc(rt_done, 1)

        @block.vector
        def _(dve):
            dve.wait_ge(silu_done, 1)
            dve.tensor_copy(c_rows[:], csil[:, :, 0:1].broadcast_to([P, KC, P])).then_inc(crow_done, 1)
            steps = [0]

            def lgs(ins):
                steps[0] += 1
                ins.then_inc(lg_step, 1)
                dve.wait_ge(lg_step, steps[0])

            dve.wait_ge(lg_act, 1)
            lgs(dve.tensor_scalar(lgt[:, 1, :], lgt[:, 0, :], -1.0, 1.0, ALU.mult, ALU.add))
            lgs(dve.tensor_scalar(lgt[:, 3, :], lgt[:, 1, :], -1.0, 1.0, ALU.mult, ALU.add))
            lgs(dve.tensor_scalar(lgt[:, 4, :], lgt[:, 3, :], 0.0, None, ALU.is_equal))
            lgs(dve.tensor_tensor(lgt[:, 3, :], lgt[:, 3, :], lgt[:, 4, :], ALU.add))
            lgs(dve.reciprocal(lgt[:, 5, :], lgt[:, 3, :]))
            lgs(dve.tensor_tensor(lgt[:, 5, :], lgt[:, 5, :], lgt[:, 0, :], ALU.mult))
            dve.wait_ge(lg_act, 2)
            lgs(dve.tensor_tensor(lgt[:, 5, :], lgt[:, 5, :], lgt[:, 2, :], ALU.mult))
            lgs(dve.tensor_tensor(lgt[:, 4, :], lgt[:, 4, :], lgt[:, 0, :], ALU.mult))
            lgs(dve.tensor_tensor(lg[:], lgt[:, 5, :], lgt[:, 4, :], ALU.subtract))

            dve.wait_ge(sq_done, 6)
            dve.tensor_scalar(ss[:, 0:6], ss[:, 0:6], 1.0 / D, EPS, ALU.mult, ALU.add).then_inc(ms_done, 1)
            dve.wait_ge(rt_done, 1)
            dve.reciprocal(rs[:, 0:6], rs[:, 0:6]).then_inc(rs_done, 1)
            dve.wait_ge(rs_done, 1)
            for tb in range(TB):
                dve.tensor_scalar(xs[:, tb, :], xs[:, tb, :], rs[:, tb:tb + 1], None, ALU.mult).then_inc(xn_done, 1)
            for tb in range(CB):
                dve.tensor_scalar(cx[:, tb, :], cx[:, tb, :], rs[:, TB + tb:TB + tb + 1], None, ALU.mult).then_inc(xn_done, 1)

            msteps = [0]

            def modulation(bank, bada, gain):
                sh = ps[:, bank, 0:2 * KC].rearrange("p (c t) -> p c t", t=2)
                sc = ps[:, bank, 2 * KC:4 * KC].rearrange("p (c t) -> p c t", t=2)
                dve.tensor_tensor(mod_b[:], sh, colp[:, bada:bada + KC].unsqueeze(2).broadcast_to([P, KC, 2]),
                                  ALU.add).then_inc(mod_step, 1)
                dve.tensor_tensor(mod_t[:], sc, colp[:, bada + KC:bada + 2 * KC].unsqueeze(2).broadcast_to([P, KC, 2]),
                                  ALU.add).then_inc(mod_step, 1)
                msteps[0] += 2
                dve.wait_ge(mod_step, msteps[0])
                dve.scalar_tensor_tensor(mod_a[:], mod_t[:], 1.0,
                                         colp[:, gain:gain + KC].unsqueeze(2).broadcast_to([P, KC, 2]),
                                         ALU.add, ALU.mult).then_inc(mod_step, 1)
                msteps[0] += 1
                dve.wait_ge(mod_step, msteps[0])

            dve.wait_ge(ada_used, 2 * KC)
            modulation(0, C_BADA, C_NPM)

            def full_of(dst, bank, width, kc, which, m, before):
                dve.wait_ge(tr_done, m + 1)
                if before:
                    dve.wait_ge(full_lo, before)
                dve.tensor_scalar(dst, ps[:, bank, 0:width], mod_a[:, kc, which:which + 1],
                                  mod_b[:, kc, which:which + 1], ALU.mult, ALU.add).then_inc(full_done, 1)

            def rest_of(dst, src, hi, m):
                dve.wait_ge(full_hi, m + 1)
                dve.tensor_tensor(dst, src, hi.bitcast(F32), ALU.subtract).then_inc(full_lo, 1)

            for m in range(2 * KC + 1):
                kc = m // 2
                if m < 2 * KC:
                    w = N if m % 2 == 0 else NCTX
                    full_of(full[:, m % 2, 0:w], 1 + m % 6, w, kc, m % 2, m, m - 1 if m >= 2 else 0)
                if m:
                    kc = (m - 1) // 2
                    if m % 2:
                        rest_of(hT_lo[:, kc, :], full[:, 0, :], hT_hi[:, kc, :], m - 1)
                    else:
                        rest_of(cT_lo[:, kc, :], full[:, 1, 0:NCTX], cT_hi[:, kc, :], m - 1)

            def rest_unit(n):
                s = split_index[n]
                dve.wait_ge(split_hi, s + 1)
                dve.tensor_tensor(ws_lo[s % SPLIT][:], raw[:, n % RAW, :], ws_hi[s % SPLIT][:].bitcast(F32),
                                  ALU.subtract).then_inc(split_lo, 1)

            rsteps = [0]

            def rope_all(t, kind):
                for tb in range(TB):
                    s = tb % 2
                    src = t[:, tb, :].rearrange("p (h a r) -> p h a r", h=HEADS, a=2)
                    one = rope_tmp[:, s, 0, :].rearrange("p (h a r) -> p h a r", h=HEADS, a=2)
                    two = rope_tmp[:, s, 1, :].rearrange("p (h a r) -> p h a r", h=HEADS, a=2)

                    def table(k):
                        return rope_sb[:, tb, kind + k, :].unsqueeze(1).broadcast_to([P, HEADS, 32])

                    if rsteps[0] >= 10:
                        dve.wait_ge(rope_step, rsteps[0] - 5)
                    elif rsteps[0]:
                        dve.wait_ge(rope_step, rsteps[0])
                    for a in range(2):
                        dve.tensor_tensor(one[:, :, a, :], src[:, :, a, :], table(0), ALU.mult).then_inc(rope_step, 1)
                        dve.tensor_tensor(two[:, :, a, :], src[:, :, 1 - a, :], table(1 + a), ALU.mult).then_inc(rope_step, 1)
                    dve.wait_ge(rope_step, rsteps[0] + 4)
                    dve.tensor_tensor(t[:, tb, :], rope_tmp[:, s, 0, :], rope_tmp[:, s, 1, :], ALU.add).then_inc(rope_step, 1)
                    rsteps[0] += 5

            for p in range(n_proj + 1):
                for j in range(4 if p < n_proj else 0):
                    rest_unit(split_units[4 * p + j])
                if p == 1:
                    dve.wait_ge(proj_taken, 6)
                    dve.wait_ge(rope_in, 16)
                    rope_all(k_sb, 3)
                if p == 3:
                    for tb in range(TB):
                        dve.wait_ge(proj_taken, 12 + tb + 1)
                        dve.tensor_tensor(f_lo[:, tb, :], ps[:, x_banks[2][tb], :], f_hi[:, tb, :].bitcast(F32),
                                          ALU.subtract).then_inc(f_rest, 1)
                if p == 4:
                    dve.wait_ge(proj_taken, 20)
                    rope_all(q_sb, 0)
                if p == 5:
                    dve.wait_ge(proj_taken, 24)
                    dve.wait_ge(gain_in, 16)
                    dve.tensor_tensor(gate[:], gate[:], ret_gain[:].unsqueeze(1).broadcast_to([P, TB, W512]),
                                      ALU.mult).then_inc(gate_done, 1)
            for m in range(4):
                dve.wait_ge(dft_r, m + 1)
                dve.tensor_tensor(dft_lo[:, 2 * m:2 * m + 2, :], dft_raw[:, 2 * m:2 * m + 2, :],
                                  dft_hi[:, 2 * m:2 * m + 2, :].bitcast(F32), ALU.subtract).then_inc(dft_l, 1)
            dve.wait_ge(dft_r, 5)
            dve.tensor_tensor(dfs_lo[:], dfs_raw[:], dfs_hi[:].bitcast(F32), ALU.subtract).then_inc(dft_l, 1)

            def rest_y(g):
                for t in range(2):
                    dve.wait_ge(y_r, 2 * g + t + 1)
                    dve.tensor_tensor(y_lo[:, g % 2, t, :], ps[:, 2 * g + t, :], y_hi[:, g % 2, t, :].bitcast(F32),
                                      ALU.subtract).then_inc(y_l, 1)

            def rest_four(g):
                dve.wait_ge(four_r, g + 1)
                dve.tensor_tensor(four_lo[:, g, :], ps[:, 2 * g, :], four_hi[:, g, :].bitcast(F32),
                                  ALU.subtract).then_inc(four_l, 1)

            dve.wait_ge(iotas, 5)
            for d in range(2):
                for jb in range(CB):
                    dve.tensor_scalar(ck_dec[:, d, jb, :], lg[:, 8 + 8 * d:16 + 8 * d], ck_pos[:, d, jb:jb + 1], None,
                                      ALU.mult).then_inc(ckd_done, 1)
            rest_y(0)
            rest_y(1)
            rest_four(0)
            rest_y(2)
            rest_four(1)
            rest_y(3)
            rest_four(2)
            rest_four(3)

            dve.wait_ge(iotas, 6)
            dve.tensor_scalar(r_fwd[:], delta[:], 0.0, None, ALU.max).then_inc(ret_step, 1)
            dve.tensor_scalar(r_bwd[:], delta[:], -1.0, 0.0, ALU.mult, ALU.max).then_inc(ret_step, 1)
            dve.wait_ge(dft1_done, 8)
            dve.wait_ge(ret_act, 1)
            for d in range(2):
                for jb in range(CB):
                    dve.tensor_tensor(ck_w[:, d, jb, :].rearrange("p (h e) -> p h e", h=HEADS),
                                      ck_sb[:, jb, :].rearrange("p (h e) -> p h e", h=HEADS),
                                      ck_dec[:, d, jb, :].unsqueeze(2).broadcast_to([P, HEADS, DH]),
                                      ALU.mult).then_inc(ckw_done, 1)

            def exponent(h):
                if h == 0:
                    dve.wait_ge(ret_step, 2)
                else:
                    dve.wait_ge(mask_done, h)
                dve.tensor_scalar(expo[:], r_bwd[:], lg[:, 16 + h:17 + h], None, ALU.mult).then_inc(ret_step, 1)
                dve.wait_ge(ret_step, 3 + h)
                dve.scalar_tensor_tensor(expo[:], r_fwd[:], lg[:, 8 + h:9 + h], expo[:], ALU.mult,
                                         ALU.add).then_inc(expo_done, 1)

            def masked(h):
                dve.wait_ge(mask_done, h + 1)
                if h >= 4:
                    dve.wait_ge(ret_done, (h - 4) // 2 + 1)
                for jb in range(TB):
                    dve.wait_ge(sc_done, 4 * h + jb + 1)
                    lo = N - P - P * jb
                    dve.tensor_tensor(scores[:, h % 4, jb, :], ps[:, jb, :], mask[:, h % 2, lo:lo + N],
                                      ALU.mult).then_inc(msc_done, 1)

            def decayed(c2):
                for d in range(2):
                    dve.wait_ge(dec_done, 2 * c2 + d + 1)
                    if c2 >= 2:
                        dve.wait_ge(ret_done, c2 - 1)
                    dve.tensor_tensor(q_dec[:, c2 % 2, d, :], qT[:, c2, :], dec_rows[:, d, :],
                                      ALU.mult).then_inc(qd_done, 1)

            exponent(0)
            dve.wait_ge(st_done, 1)
            for d in range(2):
                for a in range(2):
                    src = ps[64 * a:64 * a + 64, 4 + d, :].rearrange("p (c m) -> p c m", c=PAIRS)
                    dve.tensor_copy(s_diag[64 * a:64 * a + 64, d, :, 64 * a:64 * a + 64],
                                    src[:, :, 64 * a:64 * a + 64]).then_inc(st_taken, 1)
            for h in range(HEADS):
                if h + 1 < HEADS:
                    exponent(h + 1)
                if h % 2 == 0:
                    decayed(h // 2)
                masked(h)
            nsteps = [0]
            for ib in range(TB):
                dve.wait_ge(rsq_done, ib + 1)
                dve.tensor_reduce(ss_ret[:, ib, :], ret_tmp[:, ib % 2, :].rearrange("p (h e) -> p h e", h=HEADS), AX,
                                  ALU.add).then_inc(rss_done, 1)
            dve.wait_ge(rss_done, TB)
            dve.tensor_scalar(ss_ret[:], ss_ret[:], 1.0 / DH, EPS, ALU.mult, ALU.add).then_inc(rss_done, 1)
            dve.wait_ge(rrt_done, 1)
            dve.reciprocal(rs_ret[:], rs_ret[:]).then_inc(nrm_step, 1)
            dve.wait_ge(nrm_step, 1)
            dve.wait_ge(gate_done, 1)
            for ib in range(TB):
                m3 = mix_r[:, ib, :].rearrange("p (h e) -> p h e", h=HEADS)
                dve.tensor_tensor(m3, ps[:, 4 + ib, :].rearrange("p (h e) -> p h e", h=HEADS),
                                  rs_ret[:, ib, :].unsqueeze(2).broadcast_to([P, HEADS, DH]), ALU.mult).then_inc(nrm_step, 1)
            for ib in range(TB):
                dve.wait_ge(nrm_step, 2 + ib)
                dve.tensor_tensor(mix_r[:, ib, :], mix_r[:, ib, :], gate[:, ib, :], ALU.mult).then_inc(mixr_done, 1)
            dve.wait_ge(rows_in, 64)
            dve.wait_ge(mixr_done, TB)
            for r in range(2):
                dve.wait_ge(ada_used, 2 * KC + KC * (r + 1))
                dve.tensor_tensor(gg[:, r, :], ps[:, 2 * r:2 * r + 2, :].rearrange("p a n -> p (a n)"), row_in[:, r, :],
                                  ALU.add).then_inc(gg_step, 1)
                dve.wait_ge(gg_step, 2 * r + 1)
                dve.tensor_tensor(gg[:, r, :], gg[:, r, :], row_in[:, 2 + r, :], ALU.mult).then_inc(gg_step, 1)
            for c2 in range(PAIRS):
                dve.wait_ge(ret_r, c2 + 1)
                dve.tensor_tensor(ret_lo[:, c2, :], ps[:, c2, :], ret_hi[:, c2, :].bitcast(F32),
                                  ALU.subtract).then_inc(ret_l, 1)
            dve.wait_ge(ada_used, 6 * KC)
            modulation(4, C_BADA + 3 * KC, C_NPF)
            for m in range(8):
                rest_unit(split_units[20 + m])
            dve.wait_ge(sq_done, 14)
            dve.tensor_tensor(ss[:, 0:4], ss[:, 0:4], ss[:, 4:8], ALU.add).then_inc(ms_done, 1)
            dve.wait_ge(ms_done, 2)
            dve.tensor_scalar(ss[:, 0:4], ss[:, 0:4], 1.0 / D, EPS, ALU.mult, ALU.add).then_inc(ms_done, 1)
            dve.wait_ge(rt_done, 2)
            dve.reciprocal(rs[:, 0:4], rs[:, 0:4]).then_inc(rs_done, 1)
            dve.wait_ge(rs_done, 2)
            dve.wait_ge(x_again, 16)
            dve.wait_ge(gg_step, 4)
            for tb in range(TB):
                for half in range(2):
                    m = 2 * tb + half
                    if m >= 2:
                        dve.wait_ge(x2_step, m - 1)
                    dve.scalar_tensor_tensor(out_tmp[:, half, :], ps[:, 4 * half + tb, :], rs[:, tb:tb + 1],
                                             gg[:, 0, half * 512:half * 512 + 512], ALU.mult, ALU.mult).then_inc(y_scaled, 1)
                    dve.wait_ge(y_scaled, m + 1)
                    dve.tensor_tensor(x2[:, tb, half * 512:half * 512 + 512], x2[:, tb, half * 512:half * 512 + 512],
                                      out_tmp[:, half, :], ALU.add).then_inc(x2_step, 1)
            dve.wait_ge(sq_done, 18)
            dve.tensor_scalar(ss[:, 4:8], ss[:, 4:8], 1.0 / D, EPS, ALU.mult, ALU.add).then_inc(ms_done, 1)
            dve.wait_ge(rt_done, 3)
            dve.reciprocal(rs[:, 4:8], rs[:, 4:8]).then_inc(rs_done, 1)
            dve.wait_ge(rs_done, 3)
            for tb in range(TB):
                dve.tensor_scalar(xn2[:, tb, :], x2[:, tb, :], rs[:, 4 + tb:5 + tb], None, ALU.mult).then_inc(xn_done, 1)
            for m in range(KC + 1):
                if m < KC:
                    full_of(full2[:, m % 2, :], 1 + m % 6, N, m, 0, 2 * KC + m, 2 * KC + m - 1 if m >= 2 else 0)
                if m:
                    rest_of(hT_lo[:, m - 1, :], full2[:, (m - 1) % 2, :], hT_hi[:, m - 1, :], 2 * KC + m - 1)

            def take_s(m):
                dve.wait_ge(s_done, m + 1)
                dst = s_all[:, :, m * KEYS:(m + 1) * KEYS]
                dve.tensor_copy(dst, ps[:, 2 + m % 2, :].rearrange("p (b k) -> p b k", b=TB)).then_inc(s_taken, 1)

            for m in range(2 * PH):
                rest_unit(split_units[28 + m])
                if m >= 3:
                    take_s(m - 3)
            for m in range(2 * PH - 3, 2 * PH):
                take_s(m)

            per = 1 + 10 * PH + 5 + 1 + 5 * PH + 5 + 4 + 1 + 2 * 3 + 1
            dve.wait_ge(s_taken, 2 * PH)
            with dve.Fori(0, TB) as tb:
                n = [0]

                def step(ins, wait=True):
                    n[0] += 1
                    ins.then_inc(top_step, 1)
                    if wait:
                        dve.wait_ge(top_step, tb * per + n[0])

                flat = s_all[:].rearrange("p b k -> p (b k)")
                step(dve.tensor_copy(s_work[:].rearrange("p a h k -> p (a h k)"), flat[:, bass.ds(tb * 2048, 2048)]))

                def round_of(count, op):
                    step(dve.memset(guard[:], 0.0), False)
                    for h in range(count):
                        step(op(h), h == count - 1)

                def top16(src, vals, idx, count):
                    round_of(count, lambda h: dve.max(vals[h][:, 0:8], src[h]))
                    round_of(count, lambda h: dve.max_index(idx[h][:, 0:8], vals[h][:, 0:8], src[h]))
                    round_of(count, lambda h: dve.match_replace(src[h], vals[h][:, 0:8], src[h], NEG))
                    round_of(count, lambda h: dve.max(vals[h][:, 8:16], src[h]))
                    round_of(count, lambda h: dve.max_index(idx[h][:, 8:16], vals[h][:, 8:16], src[h]))

                hs = [(h, a) for h in range(PH) for a in range(2)]
                work = s_work[:].rearrange("p a h k -> p (a h) k")
                top16([work[:, 2 * h + a, :] for h, a in hs], [tv[:, a, h, :] for h, a in hs],
                      [ti[:, a, h, :] for h, a in hs], 2 * PH)
                step(dve.tensor_tensor(cand[:], tv[:, 0, :, :].unsqueeze(3).broadcast_to([P, PH, TOPK, TOPK]),
                                       tv[:, 1, :, :].unsqueeze(2).broadcast_to([P, PH, TOPK, TOPK]), ALU.add))
                best = tv[:, 0, :, :]
                top16([cand[:, h, :, :].rearrange("p a b -> p (a b)") for h in range(PH)],
                      [best[:, h, :] for h in range(PH)], [cp[:, h * TOPK:(h + 1) * TOPK] for h in range(PH)], PH)
                step(dve.tensor_scalar(cpa[:, 0, :], cp[:], 4, None, ALU.logical_shift_right), False)
                step(dve.tensor_scalar(cpa[:, 1, :], cp[:], 15, None, ALU.bitwise_and))
                step(dve.tensor_copy(cpf[:], cpa[:]), False)
                step(dve.tensor_copy(tif[:], ti[:]), False)
                step(dve.tensor_copy(sm[:, 0:PH], best[:, :, 0]))
                for half in range(2):
                    step(dve.tensor_tensor(eq[:].rearrange("p h k a -> p (h k) a"),
                                           cpf[:, half, :].unsqueeze(2).broadcast_to([P, PICKS, TOPK]),
                                           iota_k[:].unsqueeze(1).broadcast_to([P, PICKS, TOPK]), ALU.is_equal))
                    step(dve.tensor_tensor(eq[:], eq[:], tif[:, half, :, :].unsqueeze(2).broadcast_to([P, PH, TOPK, TOPK]),
                                           ALU.mult))
                    step(dve.tensor_reduce(picks[:, half, bass.ds(tb, 1), :].rearrange("p a k -> p (a k)"),
                                           eq[:].rearrange("p h k a -> p (h k) a"), AX, ALU.add))
                step(dve.tensor_tensor(picks[:, 2, bass.ds(tb, 1), :].rearrange("p a (h k) -> p (a h) k", h=PH), best,
                                       sm[:, 0:PH].unsqueeze(2).broadcast_to([P, PH, TOPK]), ALU.subtract))
                assert n[0] == per
            dve.wait_ge(exp_done, 1)
            dve.tensor_reduce(sm[:], picks[:, 2, :, :].rearrange("p b (h k) -> p (b h) k", h=PH), AX,
                              ALU.add).then_inc(soft_step, 1)
            dve.wait_ge(soft_step, 1)
            dve.reciprocal(sm[:], sm[:]).then_inc(soft_step, 1)
            dve.wait_ge(soft_step, 2)
            pw = picks[:, 2, :, :].rearrange("p b (h k) -> p (b h) k", h=PH)
            dve.tensor_tensor(pw, pw, sm[:].unsqueeze(2).broadcast_to([P, TB * PH, TOPK]), ALU.mult).then_inc(soft_step, 1)
            for r, c in enumerate((0, 1, 3)):
                dve.wait_ge(ptr_done, r + 1)
                dve.tensor_copy(picks_t[:, c, :], ps[:, 2 + r, :]).then_inc(ptr_taken, 1)
            dve.wait_ge(ptr_taken, 4)
            dve.tensor_tensor(picks_t[:, 3, :], picks_t[:, 3, :], picks_t[:, 2, :], ALU.subtract).then_inc(ptr_taken, 1)
            dve.wait_ge(ptr_taken, 5)

            def one_hots(q, p, first=False):
                if not first:
                    dve.wait_ge(oh_done, q + (-1))
                    dve.wait_ge(w_mm, q + (-1))
                dve.tensor_copy(cur[:, p, :, :], picks_t[:, :, bass.ds(q * TOK_STEP, TOK_STEP)]).then_inc(cur_done, 1)
                dve.wait_ge(cur_done, q + 1)
                for t in range(TOK_STEP):
                    for r in range(2):
                        dve.tensor_scalar(onehot[:, p, r, t, :], iota_e[:], cur[:, p, 0, t:t + 1],
                                          cur[:, p, 2 + r, t:t + 1], ALU.is_equal, ALU.mult)
                    last = dve.tensor_scalar(onehot[:, p, 2, t, :], iota_e[:], cur[:, p, 1, t:t + 1], None, ALU.is_equal)
                last.then_inc(oh_done, 1)

            one_hots(0, 0, True)
            one_hots(1, 1, True)
            with dve.Fori(1, PART_B // 2) as i:
                for p in range(2):
                    one_hots(2 * i + p, p)

            def coefficients(b, g_wait, buf, k, p, first=False):
                if g_wait is not None:
                    dve.wait_ge(grp_in[buf], g_wait)
                if not first:
                    dve.wait_ge(coef_l, b + (-1))
                gsrc = grp_g[:, buf, :, :].rearrange("p b t -> p (b t)")[:, bass.ds(k * N, N)]
                wsrc = grp_w[:, buf, :, bass.ds(k, 1), :].rearrange("p a o t -> p a (o t)")
                dve.tensor_tensor(coef[:, p, :].rearrange("p (a t) -> p a t", t=64),
                                  gsrc.rearrange("p (a t) -> p a t", t=64), wsrc, ALU.mult).then_inc(coef_done, 1)

            def rests(b, p):
                dve.wait_ge(v_hi, b + 1)
                dve.tensor_tensor(ws_lo[p][:], blk_raw[:, p, :], ws_hi[p][:].bitcast(F32), ALU.subtract).then_inc(v_lo, 1)
                dve.wait_ge(coef_r, b + 1)
                dve.tensor_tensor(coef_lo[:, p, :], coef[:, p, :], coef_hi[:, p, :].bitcast(F32),
                                  ALU.subtract).then_inc(coef_l, 1)

            dve.wait_ge(w_mm, PART_B)
            dve.wait_ge(grp_in[0], 32)
            for b in range(2):
                coefficients(b, None, 0, b, b, True)
                rests(b, b)
            with dve.Fori(1, GRP // 2) as i:
                for p in range(2):
                    coefficients(2 * i + p, None, 0, 2 * i + p, p)
                    rests(2 * i + p, p)

            def group(o, buf):
                dve.wait_ge(grp_in[buf], 32 * o + 32)
                dve.memset(guard[:], 0.0).then_inc(group_seen, 1)
                with dve.Fori(0, GRP // 2) as i:
                    for p in range(2):
                        b = 16 * o + 2 * i + (8 * buf + p)
                        coefficients(b, None, buf, 2 * i + p, p)
                        rests(b, p)

            group(0, 1)
            with dve.Fori(1, EB // GRP // 2) as o:
                for buf in range(2):
                    group(o, buf)

            dve.wait_ge(fsq_done, 8)
            sspair = ss[:].rearrange("p (b a) -> p b a", a=2)
            dve.tensor_tensor(sm[:, 0:4], sspair[:, :, 0], sspair[:, :, 1], ALU.add).then_inc(soft_step, 1)
            dve.wait_ge(soft_step, 4)
            dve.tensor_scalar(ss[:, 0:4], sm[:, 0:4], 1.0 / D, EPS, ALU.mult, ALU.add).then_inc(fin_act, 1)
            dve.wait_ge(rt_done, 4)
            dve.reciprocal(rs[:, 0:4], rs[:, 0:4]).then_inc(rs_done, 1)
            dve.wait_ge(rs_done, 4)
            for tb in range(TB):
                for half in range(2):
                    dve.scalar_tensor_tensor(fin[:, tb, half * 512:half * 512 + 512], ps[:, 2 * tb + half, :],
                                             rs[:, tb:tb + 1], gg[:, 1, half * 512:half * 512 + 512], ALU.mult,
                                             ALU.mult).then_inc(fin_step, 1)
            for tb in range(TB):
                for half in range(2):
                    dve.wait_ge(fin_step, 2 * TB)
                    sl = slice(half * 512, half * 512 + 512)
                    dve.tensor_tensor(fin[:, tb, sl], fin[:, tb, sl], x2[:, tb, sl], ALU.add).then_inc(fin_step, 1)

        @block.tensor
        def _(pe):
            def split_mm(o, lh, ll, rh, rl, start, stop):
                pe.matmul(o, lh, rh, start=start, stop=False, skip_group_check=True)
                pe.matmul(o, lh, rl, start=False, stop=False, skip_group_check=True)
                return pe.matmul(o, ll, rh, start=False, stop=stop, skip_group_check=True)

            def ada_columns(ns, bank):
                for m, n in enumerate(ns):
                    raw_ready(pe, n)
                    w = raw[:, n % RAW, :].rearrange("p (c n) -> p c n", c=KC)
                    for kc in range(KC):
                        last = pe.matmul(ps[:, bank, 2 * m:2 * m + 2], w[:, kc, :], csil[:, kc, :],
                                         start=kc == 0, stop=kc == KC - 1)
                    last.then_inc(ada_used, 1)

            def ada_rows(ns, bank):
                for m, n in enumerate(ns):
                    raw_ready(pe, n)
                    w = raw[:, n % RAW, :].rearrange("p (c n) -> p c n", c=KC)
                    for kc in range(KC):
                        last = pe.matmul(ps[:, bank + m // 4, (m % 4) * P:(m % 4 + 1) * P], c_rows[:, kc, :], w[:, kc, :],
                                         start=kc == 0, stop=kc == KC - 1)
                    last.then_inc(ada_used, 1)

            pe.wait_ge(silu_done, 1)
            ada_columns(range(2 * KC), 0)
            pe.wait_ge(ident_ld, 16)
            pe.wait_ge(xn_done, 6)
            for m in range(2 * KC):
                kc = m // 2
                if m >= 6:
                    pe.wait_ge(full_done, m - 5)
                for tb in range(TB if m % 2 == 0 else CB):
                    src = (xs if m % 2 == 0 else cx)[:, tb, kc * P:(kc + 1) * P]
                    last = pe.transpose(ps[:, 1 + m % 6, tb * P:(tb + 1) * P], src, ident[:])
                last.then_inc(tr_done, 1)

            def unit_k(s):
                hi = ws_hi[s % SPLIT][:].rearrange("p (c n) -> p c n", c=2)
                lo = ws_lo[s % SPLIT][:].rearrange("p (c n) -> p c n", c=2)
                return hi, lo

            pe.wait_ge(full_lo, 2 * KC)
            for p in range(n_proj):
                for j in range(4):
                    s = 4 * p + j
                    pe.wait_ge(split_lo, s + 1)
                    hi, lo = unit_k(s)
                    rows_of = [(hT_hi, hT_lo, tb, x_banks[p][tb]) for tb in range(TB)]
                    rows_of += [(cT_hi, cT_lo, cb, c_banks[p][cb]) for cb in range(len(c_banks[p]))]
                    for r, (th, tl, tb, bank) in enumerate(rows_of):
                        if j == 0 and bank_free[p][r]:
                            pe.wait_ge(proj_taken, bank_free[p][r])
                        if p == 4 and j == 0:
                            pe.wait_ge(f_rest, r + 1)
                        for kk in range(2):
                            kc = 2 * j + kk
                            last = split_mm(ps[:, bank, :], th[:, kc, tb * P:(tb + 1) * P], tl[:, kc, tb * P:(tb + 1) * P],
                                            hi[:, kk, :], lo[:, kk, :], kc == 0, kc == KC - 1)
                    last.then_inc(split_used, 1)
            for m in range(8):
                if m == 0:
                    pe.wait_ge(rope_step, 5 * TB)
                    pe.wait_ge(proj_taken, 20)
                if m == 4:
                    pe.wait_ge(rope_step, 10 * TB)
                if m >= 4:
                    pe.wait_ge(qk_taken, m - 3)
                for tb in range(TB):
                    src = (k_sb if m < 4 else q_sb)[:, tb, (m % 4) * P:(m % 4 + 1) * P]
                    last = pe.transpose(ps[:, m % 4, tb * P:(tb + 1) * P], src, ident[:])
                last.then_inc(qk_tr, 1)

            def dft1(g):
                for t in range(2):
                    bank = 2 * g + t
                    if bank < 4:
                        pe.wait_ge(qk_taken, 5 + bank)
                    else:
                        pe.wait_ge(proj_taken, 24)
                    for tb in range(TB):
                        last = split_mm(ps[:, bank, :], f_hi[:, tb, g * P:(g + 1) * P], f_lo[:, tb, g * P:(g + 1) * P],
                                        dft_hi[:, TB * t + tb, :], dft_lo[:, TB * t + tb, :], tb == 0, tb == TB - 1)
                    last.then_inc(dft1_done, 1)

            def dft2(g):
                pe.wait_ge(y_l, 2 * g + 2)
                for t in range(2):
                    last = split_mm(ps[:, 2 * g, :], dfs_hi[:, t, :], dfs_lo[:, t, :], y_hi[:, g % 2, t, :],
                                    y_lo[:, g % 2, t, :], t == 0, t == 1)
                last.then_inc(dft2_done, 1)

            pe.wait_ge(dft_l, 5)
            dft1(0)
            dft1(1)
            dft2(0)
            dft1(2)
            dft2(1)
            dft1(3)
            dft2(2)
            dft2(3)

            pe.wait_ge(ckw_done, 4)
            pe.wait_ge(four_l, 4)
            for d in range(2):
                for c2 in range(PAIRS):
                    for jb in range(CB):
                        last = pe.matmul(ps[:, 4 + d, c2 * P:(c2 + 1) * P], ck_w[:, d, jb, c2 * P:(c2 + 1) * P],
                                         cv_sb[:, jb, c2 * P:(c2 + 1) * P], start=jb == 0, stop=jb == CB - 1)
            last.then_inc(st_done, 1)

            def score(h):
                r = slice(64 * (h % 2), 64 * (h % 2) + 64)
                for jb in range(TB):
                    if h:
                        pe.wait_ge(msc_done, 4 * (h - 1) + jb + 1)
                    pe.matmul(ps[:, jb, :], kT[r, h // 2, jb * P:(jb + 1) * P], qT[r, h // 2, :], start=True,
                              stop=True).then_inc(sc_done, 1)

            def outputs(c2):
                pe.wait_ge(qd_done, 2 * c2 + 2)
                pe.wait_ge(msc_done, 8 * c2 + 8)
                if c2 == 0:
                    pe.wait_ge(st_taken, 4)
                for ib in range(TB):
                    bank = ps[:, 4 + ib, :]
                    for d in range(2):
                        pe.matmul(bank[:, c2 * P:(c2 + 1) * P], q_dec[:, c2 % 2, d, ib * P:(ib + 1) * P],
                                  s_diag[:, d, c2, :], start=d == 0, stop=False, skip_group_check=True)
                    for h in (2 * c2, 2 * c2 + 1):
                        for jb in range(TB):
                            last = pe.matmul(bank[:, h * DH:(h + 1) * DH], scores[:, h % 4, jb, ib * P:(ib + 1) * P],
                                             v_sb[:, jb, h * DH:(h + 1) * DH], start=False, stop=jb == TB - 1,
                                             skip_group_check=True)
                last.then_inc(ret_done, 1)

            for c2 in range(PAIRS + 1):
                if c2 < PAIRS:
                    score(2 * c2)
                    score(2 * c2 + 1)
                if c2:
                    outputs(c2 - 1)
            pe.wait_ge(msc_done, 4 * HEADS)
            pe.wait_ge(crow_done, 1)
            ada_rows(ada_rest[0:KC], 0)
            ada_rows(ada_rest[KC:2 * KC], 2)
            pe.wait_ge(mixr_done, TB)
            for c2 in range(PAIRS):
                pe.wait_ge(gg_step, 1 if c2 < 2 else 3)
                for ib in range(TB):
                    last = pe.transpose(ps[:, c2, ib * P:(ib + 1) * P], mix_r[:, ib, c2 * P:(c2 + 1) * P], ident[:])
                last.then_inc(mtr_done, 1)
            ada_columns(ada_rest[2 * KC:], 4)
            for half in range(2):
                for j in range(4):
                    s = 20 + 4 * half + j
                    pe.wait_ge(split_lo, s + 1)
                    hi, lo = unit_k(s)
                    for tb in range(TB):
                        if j == 0 and half == 0:
                            pe.wait_ge(ret_l, PAIRS)
                        if j == 0 and half == 1:
                            pe.wait_ge(mod_step, 6)
                        for kk in range(2):
                            kc = 2 * j + kk
                            mh, ml = (ret_hi, ret_lo) if kc < 4 else (four_hi, four_lo)
                            last = split_mm(ps[:, 4 * half + tb, :], mh[:, kc % 4, tb * P:(tb + 1) * P],
                                            ml[:, kc % 4, tb * P:(tb + 1) * P], hi[:, kk, :], lo[:, kk, :],
                                            kc == 0, kc == KC - 1)
                    last.then_inc(split_used, 1)
            pe.wait_ge(xn_done, 10)
            for m in range(KC):
                if m >= 6:
                    pe.wait_ge(full_done, 2 * KC + m - 5)
                for tb in range(TB):
                    last = pe.transpose(ps[:, 1 + m % 6, tb * P:(tb + 1) * P], xn2[:, tb, m * P:(m + 1) * P], ident[:])
                last.then_inc(tr_done, 1)

            def key_scores(m):
                pe.wait_ge(q_taken, m + 1)
                if m >= 2:
                    pe.wait_ge(s_taken, m - 1)
                for tb in range(TB):
                    last = pe.matmul(ps[:, 2 + m % 2, tb * P:(tb + 1) * P], q_t[:, m % 2, tb * P:(tb + 1) * P],
                                     keys_sb[:, m % 2, :], start=True, stop=True)
                last.then_inc(s_done, 1)

            pe.wait_ge(full_lo, 3 * KC)
            for m in range(2 * PH):
                s = 28 + m
                pe.wait_ge(split_lo, s + 1)
                if m >= 2:
                    pe.wait_ge(q_taken, m - 1)
                hi = ws_hi[s % SPLIT][:].rearrange("p (c n) -> p c n", c=KC)
                lo = ws_lo[s % SPLIT][:].rearrange("p (c n) -> p c n", c=KC)
                for kc in range(KC):
                    last = split_mm(ps[:, 6 + m % 2, :], hi[:, kc, :], lo[:, kc, :], hT_hi[:, kc, :], hT_lo[:, kc, :],
                                    kc == 0, kc == KC - 1)
                last.then_inc(split_used, 1)
                if m >= 1:
                    key_scores(m - 1)
            key_scores(2 * PH - 1)

            def products(b, p, free):
                pe.wait_ge(u_lo, b + 1)
                if free is not None:
                    pe.wait_ge(gelu_done, free)
                hi = ws_hi[p][:].rearrange("p (c n) -> p c n", c=KC)
                lo = ws_lo[p][:].rearrange("p (c n) -> p c n", c=KC)
                for kc in range(KC):
                    last = split_mm(ps[:, p, :], hi[:, kc, :], lo[:, kc, :], hT_hi[:, kc, :], hT_lo[:, kc, :],
                                    kc == 0, kc == KC - 1)
                last.then_inc(act_done, 1)

            def spread(q, p, free):
                pe.wait_ge(oh_done, q + 1)
                if free is not None:
                    pe.wait_ge(w_evac, free)
                for t in range(TOK_STEP):
                    o = ps[:, 2 + 2 * p + t // 4, (t % 4) * P:(t % 4 + 1) * P]
                    for r in range(2):
                        last = pe.matmul(o, onehot[:, p, 2, t, :], onehot[:, p, r, t, :], start=r == 0, stop=r == 1)
                last.then_inc(w_mm, 1)

            for b in range(2):
                products(b, b, None)
            with pe.Fori(1, PART_A // 2) as i:
                for p in range(2):
                    products(2 * i + p, p, 2 * i + (p - 1))
            pe.wait_ge(soft_step, 3)
            for r in range(3):
                for tb in range(TB):
                    last = pe.transpose(ps[:, 2 + r, tb * P:(tb + 1) * P], picks[:, r, tb, :], ident[:])
                last.then_inc(ptr_done, 1)
            for p in range(2):
                products(PART_A + p, p, PART_A + p - 1)
                spread(p, p, None)
            with pe.Fori(1, PART_B // 2) as i:
                for p in range(2):
                    products(2 * i + (PART_A + p), p, 2 * i + (PART_A + p - 1))
                    spread(2 * i + p, p, 4 * i + (2 * p - 2))
            with pe.Fori((PART_A + PART_B) // 2, EB // 2) as i:
                for p in range(2):
                    products(2 * i + p, p, 2 * i + (p - 1))

            def mix_experts(b, p, first=False, final=False):
                pe.wait_ge(coef_l, b + 1)
                for tb in range(TB):
                    for half in range(2):
                        tok = slice(tb * P, (tb + 1) * P)
                        col = slice(half * 512, half * 512 + 512)
                        last = split_mm(ps[:, 2 * tb + half, :], coef_hi[:, p, tok], coef_lo[:, p, tok],
                                        ws_hi[p][:, col], ws_lo[p][:, col], first, final)
                last.then_inc(v_mm, 1)

            pe.wait_ge(gelu_done, EB)
            mix_experts(0, 0, first=True)
            mix_experts(1, 1)
            with pe.Fori(1, EB // 2 - 1) as i:
                for p in range(2):
                    mix_experts(2 * i + p, p)
            mix_experts(EB - 2, 0)
            mix_experts(EB - 1, 1, final=True)


def tables():
    rows = N // GRID_W
    row_ids = np.repeat(np.arange(rows, dtype=np.float32), GRID_W)
    col_ids = np.tile(np.arange(GRID_W, dtype=np.float32), rows)
    pairs = DH // 4
    freqs = (np.float32(10000.0) ** (-np.arange(pairs, dtype=np.float32) / np.float32(pairs))).astype(np.float32)
    ang = np.concatenate([row_ids[:, None] * freqs, col_ids[:, None] * freqs], axis=-1).astype(np.float32)
    cos, sin = np.cos(ang).astype(np.float32), np.sin(ang).astype(np.float32)
    s = np.float32(DH ** -0.5)
    kinds = np.stack([cos, -sin, sin, cos * s, -sin * s, sin * s], axis=1)
    rope = np.ascontiguousarray(kinds.reshape(TB, P, ROPE_KINDS, 32).transpose(1, 0, 2, 3))
    t = np.arange(N)
    a = 2 * np.pi * (np.outer(t, t) % N) / N
    big = np.stack([np.cos(a), np.sin(a)]).reshape(2 * TB, P, N).transpose(1, 0, 2)
    c = np.arange(P)
    a = 2 * np.pi * (np.outer(c, c) % P) / P
    small = np.stack([np.cos(a), -np.sin(a)], axis=1) / 256.0
    f = np.float32
    return rope, np.ascontiguousarray(big.astype(f)), np.ascontiguousarray(small.astype(f)), np.eye(P, dtype=f)


def layout(x, c, ctx, c_ctx, w_ada, b_ada, norm_pre_mix, norm_post_mix, w_in, ret_decay_fwd, ret_decay_bwd,
           ret_norm_gain, w_out, norm_pre_ffn, norm_post_ffn, peer_w_query, peer_sub_keys_1, peer_sub_keys_2,
           peer_u, peer_v):
    def col(a, n):
        return np.asarray(a).reshape(n, P).T

    cc = np.stack([col(c[0], KC), col(c_ctx, KC)], axis=2).reshape(P, 2 * KC)
    dec = np.stack([np.asarray(ret_decay_fwd)[0], np.asarray(ret_decay_bwd)[0]])
    dec_pairs = np.repeat(dec.reshape(2, PAIRS, 2).transpose(2, 0, 1).reshape(2, 2 * PAIRS), DH, axis=0)
    dec_heads = np.broadcast_to(dec.reshape(1, 2 * HEADS), (P, 2 * HEADS))
    cols = np.concatenate([cc, col(b_ada[0], 6 * KC), col(norm_pre_mix[0], KC), col(norm_pre_ffn[0], KC), dec_pairs,
                           dec_heads], axis=1)
    b = np.asarray(b_ada)[0]
    gain = np.concatenate([np.asarray(ret_norm_gain)[0], np.asarray(ret_norm_gain)[0]])
    rows = np.stack([b[2 * D:3 * D], b[5 * D:6 * D], norm_post_mix[0], norm_post_ffn[0], gain])
    keys = np.stack([np.asarray(peer_sub_keys_1)[0].T, np.asarray(peer_sub_keys_2)[0].T], axis=1)
    u_t = np.asarray(peer_u)[0].reshape(EB, P, KC, P).transpose(0, 3, 2, 1).reshape(EB, P, D)
    rope, dft, dft_small, ident = tables()
    return {"x": np.asarray(x)[0], "ctxt": np.asarray(ctx)[0], "cols": cols, "w_ada": np.asarray(w_ada)[0],
            "rows": rows, "w_in": np.asarray(w_in)[0], "w_out": np.asarray(w_out)[0],
            "w_q": np.asarray(peer_w_query)[0], "keys": keys, "u_t": u_t, "v_nat": np.asarray(peer_v)[0],
            "rope": rope, "dft": dft, "dft_small": dft_small, "ident_in": ident}


def kernel(**inputs):
    import concourse.bacc as bacc
    from concourse.bass_utils import run_bass_kernel_spmd

    nc = bacc.Bacc("TRN2", target_bir_lowering=False, num_devices=1)
    arrays = {n: np.ascontiguousarray(a) for n, a in layout(**inputs).items()}
    args = {n: nc.dram_tensor(n, list(a.shape), F32, kind="ExternalInput").ap() for n, a in arrays.items()}
    out = nc.dram_tensor("out", [N, D], F32, kind="ExternalOutput").ap()
    g_dram = nc.dram_tensor("g_dram", [P, EB * N + 1024], F32).ap()
    w_dram = nc.dram_tensor("w_dram", [N // 64, P, EB * 64], F32).ap()
    build(nc, **args, out=out, g_dram=g_dram, w_dram=w_dram)
    r = run_bass_kernel_spmd(nc, [arrays], core_ids=[0])
    return r.results[0]["out"].reshape(1, N, D)
```

```python
from contextlib import ExitStack

import numpy as np

import concourse.bass as bass
from concourse import mybir

F32 = mybir.dt.float32
F32R = mybir.dt.float32r
U32 = mybir.dt.uint32
F16 = mybir.dt.float16
ALU = mybir.AluOpType
ACT = mybir.ActivationFunctionType
AX = mybir.AxisListType.X

P = 128
D = 1024
KC = D // P
N = 512
TB = N // P
NCTX = 256
CB = NCTX // P
GRID_W = 64
HEADS = 8
DH = 64
PAIRS = HEADS // 2
W512 = 512
GROUPS = 4
EPS = 1e-6
PH = 8
TOPK = 16
PICKS = PH * TOPK
KEYS = 128
EB = 128
NEG = -3.0e38

RAW = 4
SPLIT = 4
PART_RING = 4
OUT_ORDER = (2, 3, 0, 1)
Q_BANKS = (7, 0)
PART_A = 48
TOK_STEP = 8
PART_B = N // TOK_STEP
CHUNK = 64
CHUNK_STEPS = CHUNK // TOK_STEP
GRP = 4
BUFS = 4
AHEAD = 8
W_SCALE = 2.0 ** 14

C_C, C_BADA, C_NPM, C_NPF, C_POST, C_RET, C_DECP, C_DECH, C_END = 0, 16, 64, 72, 80, 96, 100, 108, 124
ROPE_KINDS = 6


def plan_units():
    units = []
    for piece in (1, 2, 4, 0, 3):
        units += [("in", piece * W512, j) for j in range(4)]
    for half in range(2):
        units += [("out", half * W512, j) for j in OUT_ORDER]
    units += [("q", c * P, 0) for c in range(2 * PH)]
    return units


def build(nc, x, ctxt, cols, w_ada, w_in, w_out, w_q, keys, u_t, v_nat, rope, dft, dft_small, ident_in,
          out, g_dram, w_dram):
    units = plan_units()
    n_units = len(units)

    es = ExitStack()
    with es:
        def sem(name):
            return es.enter_context(nc.semaphore(name))

        base = 16896
        K = 1024
        rA = base
        rC = rA + 32 * K
        rH = rC + 16 * K
        rD = rH + 8 * K
        rE = rD + 16 * K
        rJ = rE + 32 * K
        rF = rJ + 16 * K
        rG = rF + 16 * K
        rB = rG + 16 * K
        rI = rB + 16 * K
        rS = rI + 16 * K
        small_at = [rS]

        def at(name, offset, shape, dt=F32):
            return nc.alloc_sbuf_tensor_at(name, [P] + shape, dt, offset=offset)

        def small(name, shape, dt=F32):
            size = 4 * int(np.prod(shape))
            t = at(name, small_at[0], shape, dt)
            small_at[0] += -(-size // 64) * 64
            assert small_at[0] <= 229344
            return t

        hT_hi = at("hT_hi", rA, [KC, N], F32R)
        hT_lo = at("hT_lo", rA + 16 * K, [KC, N], F32R)
        dft_hi = at("dft_hi", rA, [2 * TB, N], F32R)
        dft_lo = at("dft_lo", rA + 16 * K, [2 * TB, N], F32R)
        q_dec = at("q_dec", rA + 4 * K, [2, 2, N])
        dec_rows = at("dec_rows", rA + 12 * K, [PAIRS, 2, P])
        ck_w = at("ck_w", rA + 16 * K, [2, CB, W512])
        state = [at("state_fwd", rA + 24 * K, [TB, PAIRS, P]), at("state_bwd", rF, [TB, PAIRS, P])]
        xs = at("xs", rC, [TB, D])
        dft_raw = at("dft_raw", rC, [2 * TB, N])
        x2 = at("x2", rC, [TB, D])
        ada_w = [at(f"ada_w{k}", rE + 8 * K * k if k < 4 else rF + 8 * K * (k - 4), [2 * D]) for k in range(KC)]
        mod_rows = at("mod_rows", rI, [2 * D])
        part_w = [at(f"part_w{i}", (rJ + 8 * K, rJ + 12 * K, rI + 8 * K, rI + 12 * K)[i], [D]) for i in range(PART_RING)]
        part_acc = [at(f"part_acc{g}", (rH if g < 2 else rF) + 4 * K * (g % 2), [D]) for g in range(4)]
        diag = at("diag", rG + 8 * K, [2, D])
        xT = at("xT", rA + 16 * K, [KC, N])
        cxT = at("cxT", rB + 8 * K, [KC, NCTX])
        gate = at("gate", rH, [TB, W512])
        gg = at("gg", rH, [2, D])
        raw = at("raw", rD, [RAW, D])
        blk_raw = at("blk_raw", rD, [2, D])
        g_buf = at("g_buf", rD + 8 * K, [2, N])
        ws_hi = [at(f"ws_hi{i}", rE + 8 * K * i, [D], F32R) for i in range(SPLIT)]
        ws_lo = [at(f"ws_lo{i}", rE + 8 * K * i + 4 * K, [D], F32R) for i in range(SPLIT)]
        y_hi = at("y_hi", rE, [2, 2, N], F32R)
        y_lo = at("y_lo", rE + 8 * K, [2, 2, N], F32R)
        scores = at("scores", rE, [HEADS, N])
        k_w = at("k_w", rE + 16 * K, [2, TB - 1, W512])
        picks = at("picks", rE + 16 * K, [3, TB, PICKS])
        onehot = at("onehot", rE + 16 * K, [2, 3, TOK_STEP, P], F16)
        rope_tmp = at("rope_tmp", rJ, [2, 2, W512])
        cx = at("cx", rJ + 8 * K, [CB, D])
        four_hi = at("four_hi", rJ, [GROUPS, N], F32R)
        four_lo = at("four_lo", rJ + 8 * K, [GROUPS, N], F32R)
        q_t = at("q_t", rJ, [2, N])
        picks_t = at("picks_t", rJ + 4 * K, [4, N])
        w_round = at("w_round", rJ + 14 * K, [N], F16)
        coef = at("coef", rE + 16 * K, [2, N])
        coef_hi = at("coef_hi", rE + 20 * K, [2, N], F32R)
        coef_lo = at("coef_lo", rE + 24 * K, [2, N], F32R)
        q_sb = at("q_sb", rF, [TB, W512])
        k_sb = at("k_sb", rF + 8 * K, [TB, W512])
        v_sb = at("v_sb", rG, [TB, W512])
        cv_sb = at("cv_sb", rG + 8 * K, [CB, W512])
        ck_sb = at("ck_sb", rG + 12 * K, [CB, W512])
        cT_hi = at("cT_hi", rB, [KC, NCTX], F32R)
        cT_lo = at("cT_lo", rB + 8 * K, [KC, NCTX], F32R)
        qT = at("qT", rB, [PAIRS, N])
        kT = at("kT", rB + 8 * K, [PAIRS, N])
        f_hi = at("f_hi", rI, [TB, W512], F32R)
        f_lo = at("f_lo", rI + 8 * K, [TB, W512], F32R)
        ret_hi = at("ret_hi", rI, [PAIRS, N], F32R)
        ret_lo = at("ret_lo", rI + 8 * K, [PAIRS, N], F32R)
        ret_sq = at("ret_sq", rI + 12 * K, [2, N])
        ret_rs = at("ret_rs", rA + 16 * K, [PAIRS, N])
        mix_r = at("mix_r", rF, [PAIRS, N])
        xn2 = at("xn2", rG, [TB, D])
        out_tmp = at("out_tmp", rF, [TB, D])
        s_all = at("s_all", rF, [TB, 2 * PH * KEYS])
        s_work = at("s_work", rB, [2, PH, KEYS])
        cand = at("cand", rB + 8 * K, [PH, TOPK, TOPK])
        eq = at("eq", rI, [PH, TOPK, TOPK])
        w_stage = at("w_stage", rF, [2, EB, CHUNK])
        grp_g = at("grp_g", rF, [BUFS, GRP, N])
        grp_w = at("grp_w", rF + 32 * K, [BUFS, N // CHUNK, GRP, CHUNK])
        fin = at("fin", rF, [TB, D])
        colp = small("colp", [C_END])
        ident = small("ident", [P])
        rope_sb = small("rope_sb", [TB, ROPE_KINDS, 32])
        csil = small("csil", [KC, 2])
        ones = small("ones", [P])
        mod2 = small("mod2", [4, KC])
        mod2_a = small("mod2_a", [KC])
        keys_sb = small("keys_sb", [2, KEYS])
        dfs_raw = small("dfs_raw", [2, P])
        dfs_hi = small("dfs_hi", [2, P], F32R)
        dfs_lo = small("dfs_lo", [2, P], F32R)
        mod_a = small("mod_a", [KC, 2])
        mod_b = small("mod_b", [KC, 2])
        mod_t = small("mod_t", [KC, 2])
        ss = small("ss", [8])
        rs = small("rs", [8])
        blocks = small("blocks", [P])
        lg = small("lg", [24])
        lgt = small("lgt", [6, 24])
        ck_pos = small("ck_pos", [2, CB])
        ck_dec = small("ck_dec", [2, CB, HEADS])
        delta = small("delta", [P])
        r_fwd = small("r_fwd", [P])
        r_bwd = small("r_bwd", [P])
        pos_rows = small("pos_rows", [2, P])
        chunk_dec = small("chunk_dec", [2, PAIRS])
        iota_b = small("iota_b", [P], F16)
        iota_k = small("iota_k", [TOPK])
        tv_at = small_at[0]
        small_at[0] += 4 * K
        mask = at("mask", tv_at, [HEADS, P])
        tv = at("tv", tv_at, [2, PH, TOPK])
        ti = at("ti", tv_at + K, [2, PH, TOPK], U32)
        tif = at("tif", tv_at + 2 * K, [2, PH, TOPK])
        cpf = at("cpf", tv_at + 3 * K, [2, PICKS])
        cur = small("cur", [2, 4, TOK_STEP])
        cp = small("cp", [PICKS], U32)
        cpa = small("cpa", [2, PICKS], U32)
        sm = small("sm", [TB * PH])
        guard = small("guard", [1])
        junk = at("junk", rJ + 4 * K, [D])
        full2 = at("full2", rI, [2, N])
        junk2 = at("junk2", rB, [2, D])

        ps = es.enter_context(nc.psum_tensor("ps", [P, 8, 512], F32))
        y_banks = ps[:].rearrange("p (t h) n -> p t (h n)", h=2)

        cols_in, ident_ld, x_in, cx_in = sem("cols_in"), sem("ident_ld"), sem("x_in"), sem("cx_in")
        rope_in, tail_in, dft_in, x_again = sem("rope_in"), sem("tail_in"), sem("dft_in"), sem("x_again")
        ada_in = [sem(f"ada_in{k}") for k in range(KC)]
        part_in = [sem(f"part_in{i}") for i in range(PART_RING)]
        raw_in = [sem(f"raw_in{i}") for i in range(RAW)]
        ada_used, split_hi, split_lo, split_used = (
            sem("ada_used"), sem("split_hi"), sem("split_lo"), sem("split_used"))
        iotas, silu_done, lg_step = sem("iotas"), sem("silu_done"), sem("lg_step")
        ada_done, rows_out, modc_done, part_done = sem("ada_done"), sem("rows_out"), sem("modc_done"), sem("part_done")
        mod2_sum, mod2_step, diag_done, gg_sum = sem("mod2_sum"), sem("mod2_step"), sem("diag_done"), sem("gg_sum")
        xt_taken, ct_taken = sem("xt_taken"), sem("ct_taken")
        lg_act = sem("lg_act")
        mod_step = sem("mod_step")
        sq_done, ms_done, rt_done, rs_done = sem("sq_done"), sem("ms_done"), sem("rt_done"), sem("rs_done")
        xn_done = sem("xn_done")
        tr_done, full_done, full_hi, full_lo = sem("tr_done"), sem("full_done"), sem("full_hi"), sem("full_lo")
        proj_taken, f_rest, rope_step = sem("proj_taken"), sem("f_rest"), sem("rope_step")
        dft_r, dft_l = sem("dft_r"), sem("dft_l")
        qk_tr, qk_taken = sem("qk_tr"), sem("qk_taken")
        dft1_done, y_r, y_l, dft2_done, four_r, four_l = (
            sem("dft1_done"), sem("y_r"), sem("y_l"), sem("dft2_done"), sem("four_r"), sem("four_l"))
        ret_step, ret_act, st_done, st_taken = sem("ret_step"), sem("ret_act"), sem("st_done"), sem("st_taken")
        kw_done, st_scaled, exp_step = sem("kw_done"), sem("st_scaled"), sem("exp_step")
        ckd_done, ckw_done = sem("ckd_done"), sem("ckw_done")
        expo_done, mask_done, sc_done, msc_done, ret_done = (
            sem("expo_done"), sem("mask_done"), sem("sc_done"), sem("msc_done"), sem("ret_done"))
        dec_done, qd_done = sem("dec_done"), sem("qd_done")
        rsq_done, rsum_done, rms_done, rrt_done, rinv_done, normed, mixr_done, ret_r, ret_l = (
            sem("rsq_done"), sem("rsum_done"), sem("rms_done"), sem("rrt_done"), sem("rinv_done"), sem("normed"),
            sem("mixr_done"), sem("ret_r"), sem("ret_l"))
        gg_step, x2_done = sem("gg_step"), [sem("x2_dve"), sem("x2_pool")]
        y_whole, ysq_done, yms_done, yrt_done, yrs_done, y_scaled = (
            sem("y_whole"), sem("ysq_done"), sem("yms_done"), sem("yrt_done"), sem("yrs_done"), sem("y_scaled"))
        xsq_done, xms_done, xrt_done, xrs_done = sem("xsq_done"), sem("xms_done"), sem("xrt_done"), sem("xrs_done")
        q_taken, s_done, s_taken = sem("q_taken"), sem("s_done"), sem("s_taken")
        top_step, exp_done, soft_step = (
            sem("top_step"), sem("exp_done"), sem("soft_step"))
        ptr_done, ptr_taken = sem("ptr_done"), sem("ptr_taken")
        blk_in = [sem("blk_in0"), sem("blk_in1")]
        u_hi, u_lo, act_done, gelu_done = sem("u_hi"), sem("u_lo"), sem("act_done"), sem("gelu_done")
        g_out = [sem("g_out0"), sem("g_out1")]
        cur_done, oh_done, w_mm, w_evac = sem("cur_done"), sem("oh_done"), sem("w_mm"), sem("w_evac")
        w_stored = [sem("w_stored0"), sem("w_stored1")]
        v_in = [sem("v_in0"), sem("v_in1")]
        v_hi, v_lo, coef_done, coef_r, coef_l, v_mm = (
            sem("v_hi"), sem("v_lo"), sem("coef_done"), sem("coef_r"), sem("coef_l"), sem("v_mm"))
        grp_in = [sem(f"grp_in{i}") for i in range(BUFS)]
        v_whole, fsq_done, fms_done, frt_done, frs_done, f_scaled, out_done = (
            sem("v_whole"), sem("fsq_done"), sem("fms_done"), sem("frt_done"), sem("frs_done"), sem("f_scaled"),
            sem("out_done"))
        fin_done = [sem("fin_dve"), sem("fin_pool")]

        dram_k = {"in": w_in, "out": w_out, "q": w_q}

        def unit_src(n):
            kind, c0, j = units[n]
            src = dram_k[kind].rearrange("(c p) n -> p c n", p=P)
            if kind == "q":
                return src[:, :, c0:c0 + P]
            return src[:, 2 * j:2 * j + 2, c0:c0 + W512]

        def unit_dst(n):
            t = raw[:, n % RAW, :]
            return t.rearrange("p (c n) -> p c n", c=KC if units[n][0] == "q" else 2)

        def raw_ready(eng, n):
            eng.wait_ge(raw_in[n % RAW], 16 * (n // RAW + 1))

        y_last = 27

        def unit_used(n):
            if n == y_last:
                return y_whole, TB
            return split_used, n + 1 if n < y_last else n

        n_proj = 5
        x_banks = [[0, 1, 2, 3], [6, 7, 0, 1], [4, 5, 6, 7], [0, 1, 2, 3], [4, 5, 6, 7]]
        c_banks = [[4, 5], [2, 3], [], [], []]
        bank_free = [[0] * 6, [0, 0, 1, 2, 3, 4], [6, 6, 7, 8], [9, 10, 11, 12], [0, 0, 0, 0]]
        parts = 4 * KC

        def part_group(i):
            return range(min(3 * i, parts), min(3 * i + 3, parts))

        block = es.enter_context(nc.Block())

        @block.sync
        def _(sp):
            def load_unit(n):
                if n >= RAW:
                    sp.wait_ge(split_lo, n - RAW + 1)
                sp.dma_start(unit_dst(n), unit_src(n)).then_inc(raw_in[n % RAW], 16)

            def load_part(u):
                if u == 0:
                    sp.wait_ge(tr_done, 2 * KC)
                if u >= PART_RING:
                    sp.wait_ge(part_done, u - PART_RING + 1)
                g, kc = divmod(u, KC)
                sp.dma_start(part_w[u % PART_RING][:], w_ada[kc * P:(kc + 1) * P, (2 + g) * D:(3 + g) * D],
                             ).then_inc(part_in[u % PART_RING], 16)

            for kc in range(KC):
                sp.dma_start(ada_w[kc][:], w_ada[kc * P:(kc + 1) * P, 0:2 * D]).then_inc(ada_in[kc], 16)
            for n in range(n_units):
                if n == 8:
                    sp.dma_start(dft_raw[:], dft).then_inc(dft_in, 16)
                if n == 20 + RAW:
                    sp.wait_ge(dft_l, 4)
                    sp.dma_start(x2[:], x.rearrange("(b p) d -> p b d", p=P)).then_inc(x_again, 16)
                if RAW <= n:
                    for u in part_group(n - RAW):
                        load_part(u)
                load_unit(n)

            def load_u(b, p, free):
                if free is not None:
                    sp.wait_ge(u_lo, free)
                sp.dma_start(blk_raw[:, p, :], u_t[bass.ds(b, 1), :, :].rearrange("a p n -> p (a n)")).then_inc(blk_in[p], 16)

            def store_g(b, p):
                sp.wait_ge(gelu_done, b + 1)
                sp.dma_start(g_dram[:, bass.ds(b * N, N)], g_buf[:, p, :]).then_inc(g_out[p], 16)

            sp.wait_ge(split_lo, n_units - 3)
            load_u(0, 0, None)
            sp.wait_ge(split_lo, n_units - 2)
            load_u(1, 1, None)
            with sp.Fori(0, PART_A // 2) as i:
                for p in range(2):
                    load_u(2 * i + (p + 2), p, 2 * i + (p + 1))
                    store_g(2 * i + p, p)

            def store_w(chunk, half, piece):
                e = EB // CHUNK_STEPS
                sp.wait_ge(w_evac, 2 * CHUNK_STEPS * chunk + 2 * CHUNK_STEPS)
                dst = w_dram[bass.ds(chunk, 1), :, :].rearrange("a p n -> p (a n)")
                sp.dma_start(dst[:, piece * (e * CHUNK):(piece + 1) * (e * CHUNK)],
                             w_stage[:, half, piece * e:(piece + 1) * e, :].rearrange("p b t -> p (b t)"),
                             ).then_inc(w_stored[half], 16)

            with sp.Fori(PART_A // 2, (PART_A + CHUNK_STEPS) // 2) as i:
                for p in range(2):
                    load_u(2 * i + (p + 2), p, 2 * i + (p + 1))
                    store_g(2 * i + p, p)
            with sp.Fori(0, N // CHUNK // 2) as o:
                for half in range(2):
                    for k in range(CHUNK_STEPS):
                        b = 2 * CHUNK_STEPS * o + (PART_A + CHUNK_STEPS * (half + 1) + k)
                        load_u(b + 2, k % 2, b + 1)
                        store_w(2 * o + half, half, k)
                        store_g(b, k % 2)

            def load_group(b, buf, k):
                g0 = b - k
                sp.dma_start(grp_g[:, buf, k, :], g_dram[:, bass.ds(b * N, N)]).then_inc(grp_in[buf], 16)
                e = N // CHUNK // GRP
                sp.dma_start(grp_w[:, buf, e * k:e * (k + 1), :, :].rearrange("p a b t -> p a (b t)"),
                             w_dram[e * k:e * (k + 1), :, bass.ds(g0 * CHUNK, GRP * CHUNK)].rearrange("a p n -> p a n"),
                             ).then_inc(grp_in[buf], 16)

            def load_v(b, p, free):
                if free is not None:
                    sp.wait_ge(v_lo, free)
                else:
                    sp.wait_ge(u_lo, EB - 2 + b + 1)
                sp.dma_start(blk_raw[:, p, :], v_nat[bass.ds(b * P, P), :]).then_inc(v_in[p], 16)

            for half in range(2):
                sp.wait_ge(w_stored[half], 16 * CHUNK_STEPS * (N // CHUNK // 2))
                sp.wait_ge(g_out[half], 8 * AHEAD)
            for k in range(AHEAD):
                b = EB - AHEAD + k
                if b + 2 < EB:
                    load_u(b + 2, k % 2, b + 1)
                else:
                    load_v(b + 2 - EB, k % 2, None)
                load_group(k, k // GRP % BUFS, k % GRP)
                store_g(b, k % 2)
            for p in range(2):
                sp.wait_ge(g_out[p], 16 * (EB // 2))

            def step_v(b, k):
                load_v(b + 2, k % 2, b + 1)
                load_group(b + AHEAD, (k + AHEAD) // GRP % BUFS, k % GRP)

            with sp.Fori(0, (EB - AHEAD) // (GRP * BUFS)) as o:
                for k in range(GRP * BUFS):
                    step_v(GRP * BUFS * o + k, k)
            for b in range((EB - AHEAD) // (GRP * BUFS) * GRP * BUFS, EB - 2):
                if b + AHEAD < EB:
                    step_v(b, b)
                else:
                    load_v(b + 2, b % 2, b + 1)

            for tb in range(TB):
                sp.wait_ge(fin_done[1 - tb % 2], tb // 2 + 1)
                sp.dma_start(out.rearrange("(b p) d -> p b d", p=P)[:, tb, :], fin[:, tb, :]).then_inc(out_done, 16)
            sp.wait_ge(out_done, 16 * TB)

        @block.gpsimd
        def _(pool):
            pool.iota(iota_b[:], [[1, P]], base=0, channel_multiplier=0,
                      allow_small_or_imprecise_dtypes=True).then_inc(iotas, 1)
            pool.iota(iota_k[:], [[1, TOPK]], base=0, channel_multiplier=0,
                      allow_small_or_imprecise_dtypes=True).then_inc(iotas, 1)
            pool.iota(ck_pos[:, 0, :], [[-P, CB]], base=NCTX - 1, channel_multiplier=-1,
                      allow_small_or_imprecise_dtypes=True).then_inc(iotas, 1)
            pool.iota(ck_pos[:, 1, :], [[P, CB]], base=0, channel_multiplier=1,
                      allow_small_or_imprecise_dtypes=True).then_inc(iotas, 1)
            pool.iota(delta[:], [[1, P]], base=0, channel_multiplier=-1,
                      allow_small_or_imprecise_dtypes=True).then_inc(iotas, 1)
            pool.iota(pos_rows[:, 0, :], [[1, P]], base=1, channel_multiplier=0,
                      allow_small_or_imprecise_dtypes=True).then_inc(iotas, 1)
            pool.iota(pos_rows[:, 1, :], [[-1, P]], base=P, channel_multiplier=0,
                      allow_small_or_imprecise_dtypes=True).then_inc(iotas, 1)
            pool.memset(ones[:], 1.0).then_inc(iotas, 1)
            pool.memset(blocks[:], 0.0).then_inc(iotas, 1)
            pool.wait_ge(iotas, 9)
            for a in range(2):
                pool.memset(blocks[64 * a:64 * a + 64, 64 * a:64 * a + 64], 1.0).then_inc(iotas, 1)
            pool.wait_ge(iotas, 11)
            pool.wait_ge(qk_tr, 8)
            pool.memset(state[1][:, 0, :, :], 0.0).then_inc(iotas, 1)
            pool.wait_ge(dft1_done, 8)
            pool.memset(state[0][:, 0, :, :], 0.0).then_inc(iotas, 1)
            pool.wait_ge(x_again, 16)
            for tb in (0, 1):
                pool.wait_ge(y_scaled, tb + 1)
                pool.tensor_tensor(x2[:, tb, :], x2[:, tb, :], out_tmp[:, tb, :], ALU.add).then_inc(x2_done[1], 1)

            def rest(b, p):
                pool.wait_ge(u_hi, b + 1)
                pool.tensor_tensor(ws_lo[p][:], blk_raw[:, p, :], ws_hi[p][:].bitcast(F32), ALU.subtract).then_inc(u_lo, 1)

            with pool.Fori(0, EB // 2) as i:
                for p in range(2):
                    rest(2 * i + p, p)
            for tb in (0, 2):
                pool.wait_ge(f_scaled, tb + 1)
                pool.tensor_tensor(fin[:, tb, :], fin[:, tb, :], x2[:, tb, :], ALU.add).then_inc(fin_done[1], 1)

        @block.scalar
        def _(act):
            act.dma_start(colp[:], cols).then_inc(cols_in, 16)
            act.dma_start(xs[:], x.rearrange("(b p) d -> p b d", p=P)).then_inc(x_in, 16)
            act.dma_start(cx[:], ctxt.rearrange("(b p) d -> p b d", p=P)).then_inc(cx_in, 16)
            act.dma_start(ident[:], ident_in).then_inc(ident_ld, 16)
            act.dma_start(rope_sb[:], rope).then_inc(rope_in, 16)
            act.dma_start(dfs_raw[:], dft_small).then_inc(tail_in, 16)
            act.dma_start(keys_sb[:], keys).then_inc(tail_in, 16)

            act.wait_ge(cols_in, 16)
            act.activation(csil[:].rearrange("p c t -> p (c t)"), colp[:, C_C:C_BADA], ACT.Silu).then_inc(silu_done, 1)
            act.activation(lgt[:, 0, :], colp[:, C_DECP:C_END], ACT.Exp).then_inc(lg_act, 1)
            act.wait_ge(lg_step, 1)
            act.activation(lgt[:, 2, :], lgt[:, 1, :], ACT.Ln).then_inc(lg_act, 1)

            def squares(srcs, to, first):
                for m, (src, bank) in enumerate(srcs):
                    if first + m:
                        act.wait_ge(sq_done, first + m)
                    act.activation(junk[:] if to is None else to, src, ACT.Square,
                                   accum_out=ss[:, bank:bank + 1]).then_inc(sq_done, 1)

            act.wait_ge(x_in, 16)
            squares([(xs[:, tb, :], tb) for tb in range(TB)], None, 0)
            act.wait_ge(cx_in, 16)
            squares([(cx[:, tb, :], TB + tb) for tb in range(CB)], None, TB)
            act.wait_ge(ms_done, 1)
            act.activation(rs[:, 0:6], ss[:, 0:6], ACT.Sqrt).then_inc(rt_done, 1)

            def round_full(src, dst, m):
                act.wait_ge(full_done, m + 1)
                act.activation(dst, src, ACT.Copy).then_inc(full_hi, 1)

            for kc in range(KC):
                act.wait_ge(tr_done, 2 * kc + 1)
                act.activation(xT[:, kc, :], ps[:, 4 + 2 * kc % 4, :], ACT.Copy).then_inc(xt_taken, 1)
            act.wait_ge(ada_done, 1)
            act.activation(mod_rows[0:2, 0:D], ps[0:2, 0:2, :].rearrange("p a n -> p (a n)"),
                           ACT.Copy).then_inc(rows_out, 1)

            def round_unit(n):
                s = n
                raw_ready(act, n)
                if s < SPLIT:
                    act.wait_ge(ada_used, s + 1)
                if 20 <= s < 20 + SPLIT:
                    act.wait_ge(*((ret_done, 2), (ret_done, 4), (st_done, 2), (st_done, 2))[s - 20])
                if s >= SPLIT:
                    act.wait_ge(*unit_used(s - SPLIT))
                act.activation(ws_hi[s % SPLIT][:], raw[:, n % RAW, :], ACT.Copy).then_inc(split_hi, 1)

            def take_piece(p):
                act.wait_ge(split_used, 4 * p + 4)
                for tb in range(TB):
                    src = ps[:, x_banks[p][tb], :]
                    dst, f = [(k_sb[:, tb, :], ACT.Copy), (v_sb[:, tb, :], ACT.Copy), (f_hi[:, tb, :], ACT.Copy),
                              (q_sb[:, tb, :], ACT.Copy), (gate[:, tb, :], ACT.Silu)][p]
                    act.activation(dst, src, f).then_inc(proj_taken, 1)
                for cb in range(CB if p < 2 else 0):
                    src = ps[:, c_banks[p][cb], :]
                    act.activation([ck_sb, cv_sb][p][:, cb, :], src, ACT.Copy,
                                   scale=[DH ** -0.5, 1.0][p]).then_inc(proj_taken, 1)

            for p in range(n_proj):
                for j in range(4):
                    round_unit(4 * p + j)
                    if p == 0:
                        for kc in range(2 * j, 2 * j + 2):
                            round_full(xT[:, kc, :], hT_hi[:, kc, :], 2 * kc)
                            round_full(cxT[:, kc, :], cT_hi[:, kc, :], 2 * kc + 1)
                if p:
                    take_piece(p - 1)
            def take_pair(m):
                act.wait_ge(qk_tr, m + 1)
                act.activation((kT if m < 4 else qT)[:, m % 4, :], ps[:, m % 4, :], ACT.Copy).then_inc(qk_taken, 1)

            def round_dft(m):
                act.activation(dft_hi[:, 2 * m:2 * m + 2, :], dft_raw[:, 2 * m:2 * m + 2, :], ACT.Copy).then_inc(dft_r, 1)

            for m in range(4):
                take_pair(m)
            act.wait_ge(dft_in, 16)
            act.wait_ge(split_used, 4 * n_proj)
            round_dft(0)
            round_dft(1)
            for m in range(4, 8):
                take_pair(m)
            round_dft(2)
            round_dft(3)
            act.wait_ge(tail_in, 32)
            act.activation(dfs_hi[:], dfs_raw[:], ACT.Copy).then_inc(dft_r, 1)
            take_piece(n_proj - 1)
            act.wait_ge(ckd_done, 4)
            act.activation(ck_dec[:], ck_dec[:], ACT.Exp).then_inc(ret_act, 1)
            act.activation(chunk_dec[:].rearrange("p d c -> p (d c)"), lg[:, 0:2 * PAIRS], ACT.Exp,
                           scale=float(P)).then_inc(ret_act, 1)
            act.wait_ge(expo_done, HEADS)
            act.activation(mask[:], mask[:], ACT.Exp).then_inc(mask_done, 1)

            def round_y(g):
                for t in range(2):
                    act.wait_ge(dft1_done, 2 * g + t + 1)
                    if g >= 2:
                        act.wait_ge(dft2_done, g - 1)
                    act.activation(y_hi[:, g % 2, t, :], ps[:, 2 * g + t, :], ACT.Copy).then_inc(y_r, 1)

            def round_four(g):
                act.wait_ge(dft2_done, g + 1)
                act.activation(four_hi[:, g, :], ps[:, 2 * g, :], ACT.Copy).then_inc(four_r, 1)

            round_y(0)
            round_y(1)
            round_four(0)
            round_y(2)
            round_four(1)
            round_y(3)
            round_four(2)
            round_four(3)

            def square(c2):
                act.wait_ge(ret_done, c2 + 1)
                if c2 >= 2:
                    act.wait_ge(rsum_done, c2 - 1)
                act.activation(ret_sq[:, c2 % 2, :], ps[:, 2 * c2 + 1, :], ACT.Square).then_inc(rsq_done, 1)

            act.wait_ge(dft1_done, 8)
            act.wait_ge(iotas, 7)
            for c2 in range(PAIRS):
                for d in range(2):
                    act.activation(dec_rows[:, c2, d, :], pos_rows[:, d, :], ACT.Exp,
                                   scale=lg[:, d * PAIRS + c2:d * PAIRS + c2 + 1]).then_inc(dec_done, 1)

            def root_ret(c2):
                act.wait_ge(rms_done, c2 + 1)
                act.activation(ret_rs[:, c2, :], ret_rs[:, c2, :], ACT.Sqrt).then_inc(rrt_done, 1)

            square(0)
            root_ret(0)
            square(1)
            round_unit(20)
            root_ret(1)
            square(2)
            root_ret(2)
            square(3)
            round_unit(21)
            root_ret(3)

            def round_ret(c2):
                act.wait_ge(mixr_done, c2 + 1)
                act.activation(ret_hi[:, c2, :], mix_r[:, c2, :], ACT.Copy).then_inc(ret_r, 1)

            round_unit(22)
            round_ret(0)
            round_ret(1)
            round_unit(23)
            round_ret(2)
            round_ret(3)
            for m in range(4):
                round_unit(24 + m)
            act.wait_ge(mixr_done, PAIRS)
            for r in range(2):
                for a in range(2):
                    act.wait_ge(gg_sum, 2 * r + a + 1)
                    act.activation(gg[:, r, a * 512:a * 512 + 512], ps[:, 4 * r + 2 * a + 1, :],
                                   ACT.Copy).then_inc(gg_step, 1)

            def square_y(tb):
                act.wait_ge(y_whole, tb + 1)
                if tb:
                    act.wait_ge(ysq_done, tb)
                act.activation(junk2[:, 0, :], y_banks[:, tb, :], ACT.Square,
                               accum_out=ss[:, tb:tb + 1]).then_inc(ysq_done, 1)

            def root_y(tb):
                act.wait_ge(yms_done, tb + 1)
                act.activation(rs[:, tb:tb + 1], ss[:, tb:tb + 1], ACT.Sqrt).then_inc(yrt_done, 1)

            def square_x(tb):
                act.wait_ge(x2_done[1 - tb // 2], tb % 2 + 1)
                if tb:
                    act.wait_ge(xsq_done, tb)
                act.activation(junk2[:, 1, :], x2[:, tb, :], ACT.Square, accum_out=ss[:, 4 + tb:5 + tb]).then_inc(xsq_done, 1)

            def root_x(tb):
                act.wait_ge(xms_done, tb + 1)
                act.activation(rs[:, 4 + tb:5 + tb], ss[:, 4 + tb:5 + tb], ACT.Sqrt).then_inc(xrt_done, 1)

            for m in range(3):
                round_unit(28 + m)
            for tb in range(TB):
                square_y(tb)
                root_y(tb)
            for tb in range(TB):
                square_x(tb)
                root_x(tb)
            for m in range(KC):
                round_full(full2[:, m % 2, :], hT_hi[:, m, :], 2 * KC + m)
            def take_q(m):
                act.wait_ge(*unit_used(28 + m))
                if m >= 2:
                    act.wait_ge(s_done, m - 1)
                act.activation(q_t[:, m % 2, :], ps[:, Q_BANKS[m % 2], :], ACT.Copy).then_inc(q_taken, 1)

            for m in range(2 * PH):
                if m >= 3:
                    round_unit(28 + m)
                if m >= 2:
                    take_q(m - 2)

            def round_u(b, p, used, used_value):
                act.wait_ge(blk_in[p], b * 8 + (16 - 8 * p))
                act.wait_ge(used, used_value)
                act.activation(ws_hi[p][:], blk_raw[:, p, :], ACT.Copy).then_inc(u_hi, 1)

            def gelu(b, p, first=False):
                act.wait_ge(act_done, b + 1)
                if not first:
                    act.wait_ge(g_out[p], b * 8 + (-8 * p))
                act.activation(g_buf[:, p, :], ps[:, p, :], ACT.Gelu).then_inc(gelu_done, 1)

            def take_w(q, p, half, t0):
                for r in range(2):
                    act.wait_ge(w_mm, q + 1)
                    dst = w_stage[:, half, :, bass.ds(t0 + 4 * r, 4)]
                    src = ps[:, 2 + 2 * p + r, :].rearrange("p (t b) -> p b t", t=4)
                    act.activation(dst, src, ACT.Copy, scale=1.0 / W_SCALE).then_inc(w_evac, 1)

            round_u(0, 0, *unit_used(n_units - 4))
            take_q(2 * PH - 2)
            round_u(1, 1, *unit_used(n_units - 3))
            take_q(2 * PH - 1)
            gelu(0, 0, True)
            round_u(2, 0, act_done, 1)
            gelu(1, 1, True)
            with act.Fori(1, PART_A // 2) as i:
                for p in range(2):
                    b = 2 * i + p
                    round_u(b + 1, 1 - p, act_done, b)
                    gelu(b, p)
            act.wait_ge(top_step, TB * (1 + 10 * PH + 5 + 1 + 5 * PH + 5 + 4 + 1 + 2 * 3 + 1))
            act.activation(picks[:, 2, :, :], picks[:, 2, :, :], ACT.Exp).then_inc(exp_done, 1)

            def part_b(o, half):
                with act.Fori(0, 4) as i:
                    for p in range(2):
                        q = 16 * o + 2 * i + (8 * half + p)
                        b = q + PART_A
                        round_u(b + 1, 1 - p, act_done, b)
                        gelu(b, p)
                        take_w(q, p, half, 16 * i + 8 * p)

            for half in range(2):
                part_b(0, half)
            with act.Fori(1, PART_B // 16) as o:
                for half in range(2):
                    act.wait_ge(w_stored[half], 16 * CHUNK_STEPS * o)
                    part_b(o, half)
            with act.Fori((PART_A + PART_B) // 2, EB // 2 - 1) as i:
                for p in range(2):
                    b = 2 * i + p
                    round_u(b + 1, 1 - p, act_done, b)
                    gelu(b, p)
            round_u(EB - 1, 1, act_done, EB - 2)
            gelu(EB - 2, 0)
            gelu(EB - 1, 1)

            def round_v(b, p, used, used_value):
                act.wait_ge(v_in[p], b * 8 + (16 - 8 * p))
                act.wait_ge(used, used_value)
                act.activation(ws_hi[p][:], blk_raw[:, p, :], ACT.Copy).then_inc(v_hi, 1)
                act.wait_ge(coef_done, b + 1)
                act.activation(coef_hi[:, p, :], coef[:, p, :], ACT.Copy).then_inc(coef_r, 1)

            for b in range(2):
                round_v(b, b, act_done, EB - 1 + b)
            with act.Fori(1, EB // 2) as i:
                for p in range(2):
                    b = 2 * i + p
                    round_v(b, p, v_mm, b + (-1))
            def root(tb):
                act.wait_ge(fms_done, tb + 1)
                act.activation(rs[:, tb:tb + 1], ss[:, tb:tb + 1], ACT.Sqrt).then_inc(frt_done, 1)

            for tb in range(TB):
                act.wait_ge(v_whole, tb + 1)
                if tb:
                    act.wait_ge(fsq_done, tb)
                act.activation(junk2[:, 0, :], ps[:, 2 * tb:2 * tb + 2, :].rearrange("p a n -> p (a n)"), ACT.Square,
                               accum_out=ss[:, tb:tb + 1]).then_inc(fsq_done, 1)
                root(tb)

        @block.vector
        def _(dve):
            dve.wait_ge(silu_done, 1)
            steps = [0]

            def lgs(ins):
                steps[0] += 1
                ins.then_inc(lg_step, 1)
                dve.wait_ge(lg_step, steps[0])

            dve.wait_ge(lg_act, 1)
            lgs(dve.tensor_scalar(lgt[:, 1, :], lgt[:, 0, :], -1.0, 1.0, ALU.mult, ALU.add))
            lgs(dve.tensor_scalar(lgt[:, 3, :], lgt[:, 1, :], -1.0, 1.0, ALU.mult, ALU.add))
            lgs(dve.tensor_scalar(lgt[:, 4, :], lgt[:, 3, :], 0.0, None, ALU.is_equal))
            lgs(dve.tensor_tensor(lgt[:, 3, :], lgt[:, 3, :], lgt[:, 4, :], ALU.add))
            lgs(dve.reciprocal(lgt[:, 5, :], lgt[:, 3, :]))
            lgs(dve.tensor_tensor(lgt[:, 5, :], lgt[:, 5, :], lgt[:, 0, :], ALU.mult))
            dve.wait_ge(lg_act, 2)
            lgs(dve.tensor_tensor(lgt[:, 5, :], lgt[:, 5, :], lgt[:, 2, :], ALU.mult))
            lgs(dve.tensor_tensor(lgt[:, 4, :], lgt[:, 4, :], lgt[:, 0, :], ALU.mult))
            lgs(dve.tensor_tensor(lg[:], lgt[:, 5, :], lgt[:, 4, :], ALU.subtract))

            dve.wait_ge(sq_done, 6)
            dve.tensor_scalar(ss[:, 0:6], ss[:, 0:6], 1.0 / D, EPS, ALU.mult, ALU.add).then_inc(ms_done, 1)
            dve.wait_ge(rt_done, 1)
            dve.reciprocal(rs[:, 0:6], rs[:, 0:6]).then_inc(rs_done, 1)
            dve.wait_ge(rs_done, 1)
            for tb in range(TB):
                dve.tensor_scalar(xs[:, tb, :], xs[:, tb, :], rs[:, tb:tb + 1], None, ALU.mult).then_inc(xn_done, 1)
            for tb in range(CB):
                dve.tensor_scalar(cx[:, tb, :], cx[:, tb, :], rs[:, TB + tb:TB + tb + 1], None, ALU.mult).then_inc(xn_done, 1)

            msteps = [0]

            def modulation(bank, bada, gain):
                sh = ps[:, bank, 0:2 * KC].rearrange("p (c t) -> p c t", t=2)
                sc = ps[:, bank, 2 * KC:4 * KC].rearrange("p (c t) -> p c t", t=2)
                dve.tensor_tensor(mod_b[:], sh, colp[:, bada:bada + KC].unsqueeze(2).broadcast_to([P, KC, 2]),
                                  ALU.add).then_inc(mod_step, 1)
                dve.tensor_tensor(mod_t[:], sc, colp[:, bada + KC:bada + 2 * KC].unsqueeze(2).broadcast_to([P, KC, 2]),
                                  ALU.add).then_inc(mod_step, 1)
                msteps[0] += 2
                dve.wait_ge(mod_step, msteps[0])
                dve.scalar_tensor_tensor(mod_a[:], mod_t[:], 1.0,
                                         colp[:, gain:gain + KC].unsqueeze(2).broadcast_to([P, KC, 2]),
                                         ALU.add, ALU.mult).then_inc(mod_step, 1)
                msteps[0] += 1
                dve.wait_ge(mod_step, msteps[0])

            for kc in range(KC):
                dve.wait_ge(tr_done, 2 * kc + 2)
                dve.tensor_copy(cxT[:, kc, :], ps[:, 4 + (2 * kc + 1) % 4, 0:NCTX]).then_inc(ct_taken, 1)
            dve.wait_ge(ada_done, 1)
            dve.tensor_copy(mod_rows[0:2, D:2 * D], ps[0:2, 2:4, :].rearrange("p a n -> p (a n)")).then_inc(rows_out, 1)
            dve.wait_ge(modc_done, 1)
            modulation(4, C_BADA, C_NPM)

            def rest_of(dst, src, hi, m):
                dve.wait_ge(full_hi, m + 1)
                dve.tensor_tensor(dst, src, hi.bitcast(F32), ALU.subtract).then_inc(full_lo, 1)

            def rest_unit(n):
                dve.wait_ge(split_hi, n + 1)
                dve.tensor_tensor(ws_lo[n % SPLIT][:], raw[:, n % RAW, :], ws_hi[n % SPLIT][:].bitcast(F32),
                                  ALU.subtract).then_inc(split_lo, 1)

            def modulated(kc):
                for m, t in ((2 * kc, xT), (2 * kc + 1, cxT)):
                    if kc == 0:
                        dve.wait_ge(xt_taken, KC)
                        dve.wait_ge(ct_taken, KC)
                    dve.tensor_scalar(t[:, kc, :], t[:, kc, :], mod_a[:, kc, m % 2:m % 2 + 1],
                                      mod_b[:, kc, m % 2:m % 2 + 1], ALU.mult, ALU.add).then_inc(full_done, 1)

            def modulated_rest(kc):
                for m, t, hi, lo in ((2 * kc, xT, hT_hi, hT_lo), (2 * kc + 1, cxT, cT_hi, cT_lo)):
                    rest_of(lo[:, kc, :], t[:, kc, :], hi[:, kc, :], m)

            def add_parts(i):
                for u in part_group(i):
                    g, kc = divmod(u, KC)
                    dve.wait_ge(part_in[u % PART_RING], 16 * (u // PART_RING + 1))
                    if kc == 0:
                        dve.tensor_scalar(part_acc[g][:], part_w[u % PART_RING][:], csil[:, kc, 0:1], None,
                                          ALU.mult).then_inc(part_done, 1)
                    else:
                        dve.wait_ge(part_done, u)
                        dve.scalar_tensor_tensor(part_acc[g][:], part_w[u % PART_RING][:], csil[:, kc, 0:1],
                                                 part_acc[g][:], ALU.mult, ALU.add).then_inc(part_done, 1)

            for j in range(4):
                if j == 0:
                    rest_unit(0)
                modulated(2 * j)
                modulated(2 * j + 1)
                modulated_rest(2 * j)
                modulated_rest(2 * j + 1)
                if j < 3:
                    rest_unit(j + 1)

            rsteps = [0]

            def rope_all(t, kind):
                for tb in range(TB):
                    s = tb % 2
                    src = t[:, tb, :].rearrange("p (h a r) -> p h a r", h=HEADS, a=2)
                    one = rope_tmp[:, s, 0, :].rearrange("p (h a r) -> p h a r", h=HEADS, a=2)
                    two = rope_tmp[:, s, 1, :].rearrange("p (h a r) -> p h a r", h=HEADS, a=2)

                    def table(k):
                        return rope_sb[:, tb, kind + k, :].unsqueeze(1).broadcast_to([P, HEADS, 32])

                    if rsteps[0] >= 10:
                        dve.wait_ge(rope_step, rsteps[0] - 5)
                    elif rsteps[0]:
                        dve.wait_ge(rope_step, rsteps[0])
                    for a in range(2):
                        dve.tensor_tensor(one[:, :, a, :], src[:, :, a, :], table(0), ALU.mult).then_inc(rope_step, 1)
                        dve.tensor_tensor(two[:, :, a, :], src[:, :, 1 - a, :], table(1 + a), ALU.mult).then_inc(rope_step, 1)
                    dve.wait_ge(rope_step, rsteps[0] + 4)
                    dve.tensor_tensor(t[:, tb, :], rope_tmp[:, s, 0, :], rope_tmp[:, s, 1, :], ALU.add).then_inc(rope_step, 1)
                    rsteps[0] += 5

            add_parts(0)
            for p in range(n_proj + 1):
                for j in range(4 if 0 < p < n_proj else 0):
                    rest_unit(4 * p + j)
                    add_parts(4 * p + j - 3)
                    if p == 4 and j == 0:
                        dve.wait_ge(mod2_sum, 1)
                        dve.tensor_tensor(mod2[:].rearrange("p g c -> p (g c)"), ps[:, 4, 0:4 * KC],
                                          colp[:, C_BADA + 2 * KC:C_BADA + 6 * KC], ALU.add).then_inc(mod2_step, 1)
                        dve.wait_ge(mod2_step, 1)
                        dve.scalar_tensor_tensor(mod2_a[:], mod2[:, 2, :], 1.0, colp[:, C_NPF:C_NPF + KC], ALU.add,
                                                 ALU.mult).then_inc(mod2_step, 1)
                        for r, g in enumerate((0, 3)):
                            dve.tensor_tensor(mod2[:, g, :], mod2[:, g, :],
                                              colp[:, C_POST + KC * r:C_POST + KC * (r + 1)],
                                              ALU.mult).then_inc(mod2_step, 1)
                if p == 1:
                    dve.wait_ge(proj_taken, 6)
                    dve.wait_ge(rope_in, 16)
                    rope_all(k_sb, 3)
                if p == 3:
                    dve.wait_ge(part_done, parts)
                    for tb in range(TB):
                        dve.wait_ge(proj_taken, 12 + tb + 1)
                        dve.tensor_tensor(f_lo[:, tb, :], ps[:, x_banks[2][tb], :], f_hi[:, tb, :].bitcast(F32),
                                          ALU.subtract).then_inc(f_rest, 1)
                if p == 4:
                    dve.wait_ge(proj_taken, 20)
                    rope_all(q_sb, 0)
            for m in range(4):
                dve.wait_ge(dft_r, m + 1)
                dve.tensor_tensor(dft_lo[:, 2 * m:2 * m + 2, :], dft_raw[:, 2 * m:2 * m + 2, :],
                                  dft_hi[:, 2 * m:2 * m + 2, :].bitcast(F32), ALU.subtract).then_inc(dft_l, 1)
            dve.wait_ge(dft_r, 5)
            dve.tensor_tensor(dfs_lo[:], dfs_raw[:], dfs_hi[:].bitcast(F32), ALU.subtract).then_inc(dft_l, 1)

            def rest_y(g):
                for t in range(2):
                    dve.wait_ge(y_r, 2 * g + t + 1)
                    dve.tensor_tensor(y_lo[:, g % 2, t, :], ps[:, 2 * g + t, :], y_hi[:, g % 2, t, :].bitcast(F32),
                                      ALU.subtract).then_inc(y_l, 1)

            def rest_four(g):
                dve.wait_ge(four_r, g + 1)
                dve.tensor_tensor(four_lo[:, g, :], ps[:, 2 * g, :], four_hi[:, g, :].bitcast(F32),
                                  ALU.subtract).then_inc(four_l, 1)

            dve.wait_ge(iotas, 7)
            for d in range(2):
                for jb in range(CB):
                    dve.tensor_scalar(ck_dec[:, d, jb, :], lg[:, 8 + 8 * d:16 + 8 * d], ck_pos[:, d, jb:jb + 1], None,
                                      ALU.mult).then_inc(ckd_done, 1)
            dve.tensor_scalar(r_fwd[:], delta[:], 0.0, None, ALU.max).then_inc(ret_step, 1)
            dve.tensor_scalar(r_bwd[:], delta[:], -1.0, 0.0, ALU.mult, ALU.max).then_inc(ret_step, 1)
            dve.wait_ge(ret_step, 2)
            for h in range(HEADS):
                dve.tensor_scalar(mask[:, h, :], r_bwd[:], lg[:, 16 + h:17 + h], None, ALU.mult).then_inc(exp_step, 1)
            for h in range(HEADS):
                dve.wait_ge(exp_step, h + 1)
                dve.scalar_tensor_tensor(mask[:, h, :], r_fwd[:], lg[:, 8 + h:9 + h], mask[:, h, :], ALU.mult,
                                         ALU.add).then_inc(expo_done, 1)

            def by_heads(t):
                return t.rearrange("p (h e) -> p h e", h=HEADS)

            def weighted_key(d, n):
                c = n if d == 0 else TB - 1 - n
                dve.tensor_tensor(by_heads(k_w[:, d, n, :]), by_heads(k_sb[:, c, :]),
                                  ck_dec[:, d, 1 - d, :].unsqueeze(2).broadcast_to([P, HEADS, DH]),
                                  ALU.mult).then_inc(kw_done, 1)

            def weighted_context(d):
                for jb in range(CB):
                    dve.tensor_tensor(by_heads(ck_w[:, d, jb, :]), by_heads(ck_sb[:, jb, :]),
                                      ck_dec[:, d, jb, :].unsqueeze(2).broadcast_to([P, HEADS, DH]),
                                      ALU.mult).then_inc(ckw_done, 1)

            dve.wait_ge(split_used, 4 * n_proj)
            dve.wait_ge(ret_act, 1)
            rest_y(0)
            weighted_key(0, 0)
            rest_y(1)
            weighted_key(0, 1)
            rest_four(0)
            weighted_key(0, 2)
            rest_y(2)
            weighted_key(1, 0)
            rest_four(1)
            weighted_key(1, 1)
            rest_y(3)
            weighted_key(1, 2)
            dve.wait_ge(dft1_done, 8)
            weighted_context(0)
            rest_four(2)
            weighted_context(1)
            rest_four(3)

            def masked(h):
                dve.wait_ge(mask_done, 1)
                dve.wait_ge(sc_done, h + 1)
                dve.tensor_tensor(scores[:, h, :].rearrange("p (c n) -> p c n", c=TB),
                                  ps[:, 2 * (h % 3), :].rearrange("p (c n) -> p c n", c=TB),
                                  mask[:, h, :].unsqueeze(1).broadcast_to([P, TB, P]), ALU.mult).then_inc(msc_done, 1)

            def blocks_of(t, a):
                return t[64 * a:64 * a + 64].rearrange("p (c m) -> p c m", c=PAIRS)[:, :, 64 * a:64 * a + 64]

            def scan(d):
                dve.wait_ge(st_done, d + 1)
                dve.wait_ge(iotas, 13)
                dve.wait_ge(ret_act, 2)
                for n in range(TB):
                    new = state[d][:, n, :, :].rearrange("p c m -> p (c m)")
                    if n:
                        dve.wait_ge(st_taken, 2 * (TB * d + n))
                        dve.tensor_tensor(state[d][:, n, :, :], state[d][:, n - 1, :, :],
                                          chunk_dec[:, d, :].unsqueeze(2).broadcast_to([P, PAIRS, P]),
                                          ALU.mult).then_inc(st_scaled, 1)
                        dve.wait_ge(st_scaled, (TB - 1) * d + n)
                    for a in range(2):
                        own = blocks_of(ps[:, 1 + 2 * n, :], a)
                        if n:
                            ins = dve.tensor_tensor(blocks_of(new, a), blocks_of(new, a), own, ALU.add)
                        else:
                            ins = dve.tensor_copy(blocks_of(new, a), own)
                        ins.then_inc(st_taken, 1)

            def mean_square(c2):
                dve.wait_ge(rsum_done, c2 + 1)
                dve.tensor_scalar(ret_rs[:, c2, :], ps[:, 6, :], 1.0 / DH, EPS, ALU.mult, ALU.add).then_inc(rms_done, 1)

            def decayed(c2):
                for d in range(2):
                    dve.wait_ge(dec_done, 2 * c2 + d + 1)
                    if c2 >= 2:
                        dve.wait_ge(ret_done, c2 - 1)
                    dve.tensor_tensor(q_dec[:, c2 % 2, d, :].rearrange("p (c n) -> p c n", c=TB),
                                      qT[:, c2, :].rearrange("p (c n) -> p c n", c=TB),
                                      dec_rows[:, c2, d, :].unsqueeze(1).broadcast_to([P, TB, P]),
                                      ALU.mult).then_inc(qd_done, 1)

            scan(0)
            masked(0)
            masked(1)
            masked(2)
            masked(3)
            masked(4)
            decayed(0)
            scan(1)
            masked(5)
            decayed(1)
            masked(6)
            masked(7)
            decayed(2)

            def norm(pairs):
                for c2 in pairs:
                    dve.wait_ge(rinv_done, c2 + 1)
                    dve.tensor_tensor(mix_r[:, c2, :], ps[:, 2 * c2 + 1, :], ret_rs[:, c2, :], ALU.mult).then_inc(normed, 1)
                for c2 in pairs:
                    dve.wait_ge(normed, c2 + 1)
                    dve.scalar_tensor_tensor(mix_r[:, c2, :], mix_r[:, c2, :], colp[:, C_RET + c2:C_RET + c2 + 1],
                                             gate[:, c2, :], ALU.mult, ALU.mult).then_inc(mixr_done, 1)

            def norm_rest(pairs):
                for c2 in pairs:
                    dve.wait_ge(ret_r, c2 + 1)
                    dve.tensor_tensor(ret_lo[:, c2, :], mix_r[:, c2, :], ret_hi[:, c2, :].bitcast(F32),
                                      ALU.subtract).then_inc(ret_l, 1)

            def inverse(c2):
                dve.wait_ge(rrt_done, c2 + 1)
                dve.reciprocal(ret_rs[:, c2, :], ret_rs[:, c2, :]).then_inc(rinv_done, 1)

            mean_square(0)
            decayed(3)
            inverse(0)
            rest_unit(20)
            mean_square(1)
            inverse(1)
            mean_square(2)
            mean_square(3)
            rest_unit(21)
            norm((0, 1))
            inverse(2)
            norm_rest((0, 1))
            rest_unit(22)
            inverse(3)
            norm((2, 3))
            norm_rest((2, 3))
            rest_unit(23)
            dve.wait_ge(mod2_step, 4)
            for r, g in enumerate((0, 3)):
                dve.tensor_tensor(diag[:, r, :].rearrange("p (c n) -> p c n", c=KC),
                                  ident[:].unsqueeze(1).broadcast_to([P, KC, P]),
                                  mod2[:, g, :].unsqueeze(2).broadcast_to([P, KC, P]), ALU.mult).then_inc(diag_done, 1)
            for m in range(4, 8):
                rest_unit(20 + m)
            def mean_y(tb):
                dve.wait_ge(ysq_done, tb + 1)
                dve.tensor_scalar(ss[:, tb:tb + 1], ss[:, tb:tb + 1], 1.0 / D, EPS, ALU.mult, ALU.add).then_inc(yms_done, 1)

            def mean_x(tb):
                dve.wait_ge(xsq_done, tb + 1)
                dve.tensor_scalar(ss[:, 4 + tb:5 + tb], ss[:, 4 + tb:5 + tb], 1.0 / D, EPS, ALU.mult,
                                  ALU.add).then_inc(xms_done, 1)
                dve.wait_ge(xrt_done, tb + 1)
                dve.reciprocal(rs[:, 4 + tb:5 + tb], rs[:, 4 + tb:5 + tb]).then_inc(xrs_done, 1)

            for m in range(3):
                rest_unit(28 + m)
            dve.wait_ge(x_again, 16)
            dve.wait_ge(gg_step, 4)
            mean_y(0)
            for tb in range(TB):
                if tb + 1 < TB - 1:
                    mean_y(tb + 1)
                dve.wait_ge(yrt_done, tb + 1)
                dve.reciprocal(rs[:, tb:tb + 1], rs[:, tb:tb + 1]).then_inc(yrs_done, 1)
                dve.wait_ge(yrs_done, tb + 1)
                dve.scalar_tensor_tensor(out_tmp[:, tb, :], y_banks[:, tb, :], rs[:, tb:tb + 1], gg[:, 0, :], ALU.mult,
                                         ALU.mult).then_inc(y_scaled, 1)
                if tb >= 2:
                    dve.wait_ge(y_scaled, tb + 1)
                    dve.tensor_tensor(x2[:, tb, :], x2[:, tb, :], out_tmp[:, tb, :], ALU.add).then_inc(x2_done[0], 1)
                if tb == TB - 2:
                    mean_y(TB - 1)
            for tb in range(TB):
                mean_x(tb)
                dve.wait_ge(xrs_done, tb + 1)
                dve.tensor_scalar(xn2[:, tb, :], x2[:, tb, :], rs[:, 4 + tb:5 + tb], None, ALU.mult).then_inc(xn_done, 1)
            for m in range(KC + 1):
                if m < KC:
                    dve.wait_ge(tr_done, 2 * KC + m + 1)
                    if m >= 2:
                        dve.wait_ge(full_lo, 2 * KC + m - 1)
                    dve.tensor_scalar(full2[:, m % 2, :], ps[:, 1 + m % 6, :], mod2_a[:, m:m + 1], mod2[:, 1, m:m + 1],
                                      ALU.mult, ALU.add).then_inc(full_done, 1)
                if m:
                    rest_of(hT_lo[:, m - 1, :], full2[:, (m - 1) % 2, :], hT_hi[:, m - 1, :], 2 * KC + m - 1)

            def take_s(m):
                dve.wait_ge(s_done, m + 1)
                dst = s_all[:, :, m * KEYS:(m + 1) * KEYS]
                dve.tensor_copy(dst, ps[:, 2 + m % 2, :].rearrange("p (b k) -> p b k", b=TB)).then_inc(s_taken, 1)

            for m in range(2 * PH):
                if m >= 3:
                    rest_unit(28 + m)
                if m >= 3:
                    take_s(m - 3)
            for m in range(2 * PH - 3, 2 * PH):
                take_s(m)

            per = 1 + 10 * PH + 5 + 1 + 5 * PH + 5 + 4 + 1 + 2 * 3 + 1
            dve.wait_ge(s_taken, 2 * PH)
            with dve.Fori(0, TB) as tb:
                n = [0]

                def step(ins, wait=True):
                    n[0] += 1
                    ins.then_inc(top_step, 1)
                    if wait:
                        dve.wait_ge(top_step, tb * per + n[0])

                flat = s_all[:].rearrange("p b k -> p (b k)")
                step(dve.tensor_copy(s_work[:].rearrange("p a h k -> p (a h k)"), flat[:, bass.ds(tb * 2048, 2048)]))

                def round_of(count, op):
                    step(dve.memset(guard[:], 0.0), False)
                    for h in range(count):
                        step(op(h), h == count - 1)

                def top16(src, vals, idx, count):
                    round_of(count, lambda h: dve.max(vals[h][:, 0:8], src[h]))
                    round_of(count, lambda h: dve.max_index(idx[h][:, 0:8], vals[h][:, 0:8], src[h]))
                    round_of(count, lambda h: dve.match_replace(src[h], vals[h][:, 0:8], src[h], NEG))
                    round_of(count, lambda h: dve.max(vals[h][:, 8:16], src[h]))
                    round_of(count, lambda h: dve.max_index(idx[h][:, 8:16], vals[h][:, 8:16], src[h]))

                hs = [(h, a) for h in range(PH) for a in range(2)]
                work = s_work[:].rearrange("p a h k -> p (a h) k")
                top16([work[:, 2 * h + a, :] for h, a in hs], [tv[:, a, h, :] for h, a in hs],
                      [ti[:, a, h, :] for h, a in hs], 2 * PH)
                step(dve.tensor_tensor(cand[:], tv[:, 0, :, :].unsqueeze(3).broadcast_to([P, PH, TOPK, TOPK]),
                                       tv[:, 1, :, :].unsqueeze(2).broadcast_to([P, PH, TOPK, TOPK]), ALU.add))
                best = tv[:, 0, :, :]
                top16([cand[:, h, :, :].rearrange("p a b -> p (a b)") for h in range(PH)],
                      [best[:, h, :] for h in range(PH)], [cp[:, h * TOPK:(h + 1) * TOPK] for h in range(PH)], PH)
                step(dve.tensor_scalar(cpa[:, 0, :], cp[:], 4, None, ALU.logical_shift_right), False)
                step(dve.tensor_scalar(cpa[:, 1, :], cp[:], 15, None, ALU.bitwise_and))
                step(dve.tensor_copy(cpf[:], cpa[:]), False)
                step(dve.tensor_copy(tif[:], ti[:]), False)
                step(dve.tensor_copy(sm[:, 0:PH], best[:, :, 0]))
                for half in range(2):
                    step(dve.tensor_tensor(eq[:].rearrange("p h k a -> p (h k) a"),
                                           cpf[:, half, :].unsqueeze(2).broadcast_to([P, PICKS, TOPK]),
                                           iota_k[:].unsqueeze(1).broadcast_to([P, PICKS, TOPK]), ALU.is_equal))
                    step(dve.tensor_tensor(eq[:], eq[:], tif[:, half, :, :].unsqueeze(2).broadcast_to([P, PH, TOPK, TOPK]),
                                           ALU.mult))
                    step(dve.tensor_reduce(picks[:, half, bass.ds(tb, 1), :].rearrange("p a k -> p (a k)"),
                                           eq[:].rearrange("p h k a -> p (h k) a"), AX, ALU.add))
                step(dve.tensor_tensor(picks[:, 2, bass.ds(tb, 1), :].rearrange("p a (h k) -> p (a h) k", h=PH), best,
                                       sm[:, 0:PH].unsqueeze(2).broadcast_to([P, PH, TOPK]), ALU.subtract))
                assert n[0] == per
            dve.wait_ge(exp_done, 1)
            dve.tensor_reduce(sm[:], picks[:, 2, :, :].rearrange("p b (h k) -> p (b h) k", h=PH), AX,
                              ALU.add).then_inc(soft_step, 1)
            dve.wait_ge(soft_step, 1)
            dve.reciprocal(sm[:], sm[:]).then_inc(soft_step, 1)
            dve.wait_ge(soft_step, 2)
            pw = picks[:, 2, :, :].rearrange("p b (h k) -> p (b h) k", h=PH)
            dve.tensor_tensor(pw, pw, sm[:].unsqueeze(2).broadcast_to([P, TB * PH, TOPK]), ALU.mult).then_inc(soft_step, 1)
            for r in range(2):
                dve.wait_ge(ptr_done, r + 1)
                dve.tensor_copy(picks_t[:, r, :], ps[:, 2 + r, :]).then_inc(ptr_taken, 1)
            dve.wait_ge(ptr_done, 3)
            dve.tensor_scalar(picks_t[:, 3, :], ps[:, 4, :], W_SCALE, None, ALU.mult).then_inc(ptr_taken, 1)
            dve.wait_ge(ptr_taken, 3)
            dve.tensor_copy(w_round[:], picks_t[:, 3, :]).then_inc(ptr_taken, 1)
            dve.wait_ge(ptr_taken, 4)
            dve.tensor_copy(picks_t[:, 2, :], w_round[:]).then_inc(ptr_taken, 1)
            dve.tensor_tensor(picks_t[:, 3, :], picks_t[:, 3, :], w_round[:], ALU.subtract).then_inc(ptr_taken, 1)
            dve.wait_ge(ptr_taken, 6)

            def one_hots(q, p, first=False):
                if not first:
                    dve.wait_ge(oh_done, q + (-1))
                    dve.wait_ge(w_mm, q + (-1))
                dve.tensor_copy(cur[:, p, :, :], picks_t[:, :, bass.ds(q * TOK_STEP, TOK_STEP)]).then_inc(cur_done, 1)
                dve.wait_ge(cur_done, q + 1)
                for t in range(TOK_STEP):
                    for r in range(2):
                        dve.tensor_scalar(onehot[:, p, r, t, :], iota_b[:], cur[:, p, 0, t:t + 1],
                                          cur[:, p, 2 + r, t:t + 1], ALU.is_equal, ALU.mult)
                    last = dve.tensor_scalar(onehot[:, p, 2, t, :], iota_b[:], cur[:, p, 1, t:t + 1], None,
                                             ALU.is_equal)
                last.then_inc(oh_done, 1)

            one_hots(0, 0, True)
            one_hots(1, 1, True)
            with dve.Fori(1, PART_B // 2) as i:
                for p in range(2):
                    one_hots(2 * i + p, p)

            def coefficients(b, group_use, buf, k, first=False):
                p = k % 2
                if k == 0:
                    dve.wait_ge(grp_in[buf], group_use)
                if not first:
                    dve.wait_ge(coef_l, b + (-1))
                dve.tensor_tensor(coef[:, p, :].rearrange("p (a t) -> p a t", t=CHUNK),
                                  grp_g[:, buf, k, :].rearrange("p (a t) -> p a t", t=CHUNK),
                                  grp_w[:, buf, :, k, :], ALU.mult).then_inc(coef_done, 1)

            def rests(b, p):
                dve.wait_ge(v_hi, b + 1)
                dve.tensor_tensor(ws_lo[p][:], blk_raw[:, p, :], ws_hi[p][:].bitcast(F32), ALU.subtract).then_inc(v_lo, 1)
                dve.wait_ge(coef_r, b + 1)
                dve.tensor_tensor(coef_lo[:, p, :], coef[:, p, :], coef_hi[:, p, :].bitcast(F32),
                                  ALU.subtract).then_inc(coef_l, 1)

            def groups(o, first):
                for buf in range(BUFS):
                    for k in range(GRP):
                        n = buf * GRP + k
                        b = GRP * BUFS * o + n
                        coefficients(b, 32 * GRP * o + 32 * GRP, buf, k, first and n < 2)
                        rests(b, k % 2)

            dve.wait_ge(w_mm, PART_B)
            groups(0, True)
            with dve.Fori(1, EB // (GRP * BUFS)) as o:
                groups(o, False)

            for tb in range(TB):
                dve.wait_ge(fsq_done, tb + 1)
                dve.tensor_scalar(ss[:, tb:tb + 1], ss[:, tb:tb + 1], 1.0 / D, EPS, ALU.mult, ALU.add).then_inc(fms_done, 1)
                dve.wait_ge(frt_done, tb + 1)
                dve.reciprocal(rs[:, tb:tb + 1], rs[:, tb:tb + 1]).then_inc(frs_done, 1)
                dve.wait_ge(frs_done, tb + 1)
                dve.scalar_tensor_tensor(fin[:, tb, :], ps[:, 2 * tb:2 * tb + 2, :].rearrange("p a n -> p (a n)"),
                                         rs[:, tb:tb + 1], gg[:, 1, :], ALU.mult, ALU.mult).then_inc(f_scaled, 1)
                if tb % 2:
                    dve.wait_ge(f_scaled, tb + 1)
                    dve.tensor_tensor(fin[:, tb, :], fin[:, tb, :], x2[:, tb, :], ALU.add).then_inc(fin_done[0], 1)

        @block.tensor
        def _(pe):
            def split_mm(o, lh, ll, rh, rl, start, stop):
                pe.matmul(o, lh, rh, start=start, stop=False, skip_group_check=True)
                pe.matmul(o, lh, rl, start=False, stop=False, skip_group_check=True)
                return pe.matmul(o, ll, rh, start=False, stop=stop, skip_group_check=True)

            def ada_chunk(kc):
                pe.wait_ge(ada_in[kc], 16)
                for n in range(4):
                    last = pe.matmul(ps[0:2, n, :], csil[:, kc, :], ada_w[kc][:, n * 512:(n + 1) * 512],
                                     start=kc == 0, stop=kc == KC - 1)
                last.then_inc(ada_used, 1)

            def transposed(kc):
                for m in (2 * kc, 2 * kc + 1):
                    if m >= 4:
                        pe.wait_ge(ct_taken if m % 2 else xt_taken, kc - 1)
                    for tb in range(CB if m % 2 else TB):
                        src = (cx if m % 2 else xs)[:, tb, kc * P:(kc + 1) * P]
                        last = pe.transpose(ps[:, 4 + m % 4, tb * P:(tb + 1) * P], src, ident[:])
                    last.then_inc(tr_done, 1)

            pe.wait_ge(silu_done, 1)
            for kc in range(4):
                ada_chunk(kc)
            pe.wait_ge(ident_ld, 16)
            pe.wait_ge(xn_done, 6)
            for kc in range(4):
                transposed(kc)
            ada_chunk(4)
            ada_chunk(5)
            for kc in range(4, KC):
                transposed(kc)
            ada_chunk(6)
            pe.wait_ge(ada_in[KC - 1], 16)
            for n in range(4):
                last = pe.matmul(ps[0:2, n, :], csil[:, KC - 1, :], ada_w[KC - 1][:, n * 512:(n + 1) * 512],
                                 start=False, stop=True)
            last.then_inc(ada_done, 1)
            pe.wait_ge(rows_out, 2)
            pe.wait_ge(xt_taken, KC - 1)
            for ch in range(2 * KC):
                last = pe.transpose(ps[:, 4, 2 * ch:2 * ch + 2], mod_rows[0:2, ch * P:(ch + 1) * P], ident[0:2, 0:2])
            last.then_inc(modc_done, 1)

            def unit_k(s):
                hi = ws_hi[s % SPLIT][:].rearrange("p (c n) -> p c n", c=2)
                lo = ws_lo[s % SPLIT][:].rearrange("p (c n) -> p c n", c=2)
                return hi, lo

            def transpose_pair(m):
                if m >= 4:
                    pe.wait_ge(qk_taken, m - 3)
                for tb in range(TB):
                    src = (k_sb if m < 4 else q_sb)[:, tb, (m % 4) * P:(m % 4 + 1) * P]
                    last = pe.transpose(ps[:, m % 4, tb * P:(tb + 1) * P], src, ident[:])
                last.then_inc(qk_tr, 1)

            def sum_parts():
                pe.wait_ge(part_done, parts)
                pe.wait_ge(iotas, 8)
                pe.wait_ge(proj_taken, 16)
                pe.wait_ge(f_rest, TB)
                for g in range(4):
                    for c in range(KC):
                        last = pe.matmul(ps[:, 4, g * KC + c:g * KC + c + 1], part_acc[g][:, c * P:(c + 1) * P],
                                         ones[:, 0:1], start=True, stop=True)
                last.then_inc(mod2_sum, 1)

            for p in range(n_proj):
                for j in range(4):
                    s = 4 * p + j
                    pe.wait_ge(split_lo, s + 1)
                    if p == 0:
                        pe.wait_ge(full_lo, 4 * j + 4)
                    if p == 3 and j == 3:
                        sum_parts()
                    if p == 4 and j == 2:
                        pe.wait_ge(rope_step, 5 * TB)
                        pe.wait_ge(proj_taken, 20)
                        for m in range(4):
                            transpose_pair(m)
                    hi, lo = unit_k(s)
                    rows_of = [(hT_hi, hT_lo, tb, x_banks[p][tb]) for tb in range(TB)]
                    rows_of += [(cT_hi, cT_lo, cb, c_banks[p][cb]) for cb in range(len(c_banks[p]))]
                    for r, (th, tl, tb, bank) in enumerate(rows_of):
                        if j == 0 and bank_free[p][r]:
                            pe.wait_ge(proj_taken, bank_free[p][r])
                        if p == 4 and j == 0 and r == 0:
                            pe.wait_ge(mod2_step, 1)
                        for kk in range(2):
                            kc = 2 * j + kk
                            if p == 4:
                                col = slice(tb * P, (tb + 1) * P)
                                last = split_mm(ps[:, bank, :], hi[:, kk, col], lo[:, kk, col], th[:, kc, :],
                                                tl[:, kc, :], kc == 0, kc == KC - 1)
                                continue
                            last = split_mm(ps[:, bank, :], th[:, kc, tb * P:(tb + 1) * P], tl[:, kc, tb * P:(tb + 1) * P],
                                            hi[:, kk, :], lo[:, kk, :], kc == 0, kc == KC - 1)
                    last.then_inc(split_used, 1)
            pe.wait_ge(rope_step, 10 * TB)
            for m in range(4, 8):
                transpose_pair(m)

            def dft1(g):
                for t in range(2):
                    bank = 2 * g + t
                    if g == 0:
                        pe.wait_ge(dft_l, 2 * t + 2)
                    if bank < 4:
                        pe.wait_ge(qk_taken, 5 + bank)
                    else:
                        pe.wait_ge(proj_taken, 24)
                    for tb in range(TB):
                        last = split_mm(ps[:, bank, :], f_hi[:, tb, g * P:(g + 1) * P], f_lo[:, tb, g * P:(g + 1) * P],
                                        dft_hi[:, TB * t + tb, :], dft_lo[:, TB * t + tb, :], tb == 0, tb == TB - 1)
                    last.then_inc(dft1_done, 1)

            def dft2(g):
                pe.wait_ge(y_l, 2 * g + 2)
                for t in range(2):
                    last = split_mm(ps[:, 2 * g, :], dfs_hi[:, t, :], dfs_lo[:, t, :], y_hi[:, g % 2, t, :],
                                    y_lo[:, g % 2, t, :], t == 0, t == 1)
                last.then_inc(dft2_done, 1)

            dft1(0)
            dft1(1)
            pe.wait_ge(dft_l, 5)
            dft2(0)
            dft1(2)
            dft2(1)
            dft1(3)
            dft2(2)
            dft2(3)

            def states(d):
                pe.wait_ge(ckw_done, 4)
                pe.wait_ge(kw_done, (TB - 1) * (d + 1))
                if d:
                    pe.wait_ge(st_taken, 2 * TB)
                for c2 in range(PAIRS):
                    col = slice(c2 * P, (c2 + 1) * P)
                    for jb in range(CB):
                        pe.matmul(ps[:, 1, col], ck_w[:, d, jb, col], cv_sb[:, jb, col], start=jb == 0,
                                  stop=jb == CB - 1)
                for n in range(TB - 1):
                    for c2 in range(PAIRS):
                        col = slice(c2 * P, (c2 + 1) * P)
                        last = pe.matmul(ps[:, 3 + 2 * n, col], k_w[:, d, n, col],
                                         v_sb[:, n if d == 0 else TB - 1 - n, col], start=True, stop=True)
                last.then_inc(st_done, 1)

            def score(h):
                r = slice(64 * (h % 2), 64 * (h % 2) + 64)
                if h >= 3:
                    pe.wait_ge(msc_done, h - 2)
                for c in range(TB):
                    tok = slice(c * P, (c + 1) * P)
                    last = pe.matmul(ps[:, 2 * (h % 3), tok], kT[r, h // 2, tok], qT[r, h // 2, tok], start=True,
                                     stop=True)
                last.then_inc(sc_done, 1)

            def outputs(c2):
                bank = ps[:, 2 * c2 + 1, :]
                pe.wait_ge(qd_done, 2 * c2 + 2)
                pe.wait_ge(st_taken, 4 * TB)
                for d in range(2):
                    for c in range(TB):
                        tok = slice(c * P, (c + 1) * P)
                        pe.matmul(bank[:, tok], state[d][:, c if d == 0 else TB - 1 - c, c2, :],
                                  q_dec[:, c2 % 2, d, tok], start=d == 0 and c == 0, stop=False,
                                  skip_group_check=True)
                pe.wait_ge(msc_done, 2 * c2 + 2)
                for h in (2 * c2, 2 * c2 + 1):
                    a = h % 2
                    for c in range(TB):
                        tok = slice(c * P, (c + 1) * P)
                        last = pe.matmul(ps[64 * a:64 * a + 64, 2 * c2 + 1, tok], v_sb[:, c, h * DH:(h + 1) * DH],
                                         scores[:, h, tok], start=False, stop=True, skip_group_check=True)
                last.then_inc(ret_done, 1)

            def sum_squares(c2):
                pe.wait_ge(rsq_done, c2 + 1)
                if c2:
                    pe.wait_ge(rms_done, c2)
                pe.matmul(ps[:, 6, :], blocks[:], ret_sq[:, c2 % 2, :], start=True, stop=True).then_inc(rsum_done, 1)

            pe.wait_ge(iotas, 11)
            pe.wait_ge(four_l, 4)
            states(0)
            for h in range(3):
                score(h)
            score(3)
            score(4)
            states(1)
            score(5)
            outputs(0)
            score(6)
            score(7)
            sum_squares(0)
            outputs(1)
            outputs(2)
            sum_squares(1)
            outputs(3)
            sum_squares(2)
            sum_squares(3)

            for half in range(2):
                if half == 1:
                    pe.wait_ge(diag_done, 2)
                    for r in range(2):
                        for a in range(2):
                            pe.matmul(ps[:, 4 * r + 2 * a + 1, :], ones[:], diag[:, r, a * 512:a * 512 + 512],
                                      start=True, stop=True).then_inc(gg_sum, 1)
                for n, j in enumerate(OUT_ORDER):
                    s = 20 + 4 * half + n
                    pe.wait_ge(split_lo, s + 1)
                    if half == 0 and n == 0:
                        pe.wait_ge(rms_done, PAIRS)
                    if half == 0 and j < 2:
                        pe.wait_ge(ret_l, 2 * j + 2)
                    if half == 1 and n == 0:
                        pe.wait_ge(gg_step, 4)
                    hi, lo = unit_k(s)
                    for tb in range(TB):
                        for kk in range(2):
                            kc = 2 * j + kk
                            mh, ml = (ret_hi, ret_lo) if kc < 4 else (four_hi, four_lo)
                            last = split_mm(ps[:, 2 * tb + half, :], mh[:, kc % 4, tb * P:(tb + 1) * P],
                                            ml[:, kc % 4, tb * P:(tb + 1) * P], hi[:, kk, :], lo[:, kk, :],
                                            n == 0 and kk == 0, n == 3 and kk == 1)
                        if half == 1 and n == 3:
                            last.then_inc(y_whole, 1)
                    if half == 0 or n < 3:
                        last.then_inc(split_used, 1)
            pe.wait_ge(xn_done, 10)
            for m in range(KC):
                if m >= 6:
                    pe.wait_ge(full_done, 2 * KC + m - 5)
                for tb in range(TB):
                    last = pe.transpose(ps[:, 1 + m % 6, tb * P:(tb + 1) * P], xn2[:, tb, m * P:(m + 1) * P], ident[:])
                last.then_inc(tr_done, 1)

            def key_scores(m):
                pe.wait_ge(q_taken, m + 1)
                if m >= 2:
                    pe.wait_ge(s_taken, m - 1)
                for tb in range(TB):
                    last = pe.matmul(ps[:, 2 + m % 2, tb * P:(tb + 1) * P], q_t[:, m % 2, tb * P:(tb + 1) * P],
                                     keys_sb[:, m % 2, :], start=True, stop=True)
                last.then_inc(s_done, 1)

            def query_part(m, kc):
                s = 28 + m
                hi = ws_hi[s % SPLIT][:].rearrange("p (c n) -> p c n", c=KC)
                lo = ws_lo[s % SPLIT][:].rearrange("p (c n) -> p c n", c=KC)
                last = split_mm(ps[:, Q_BANKS[m % 2], :], hi[:, kc, :], lo[:, kc, :], hT_hi[:, kc, :],
                                hT_lo[:, kc, :], kc == 0, kc == KC - 1)
                if kc == KC - 1:
                    last.then_inc(split_used, 1)

            pe.wait_ge(split_lo, 28 + 2)
            for kc in range(KC):
                pe.wait_ge(full_lo, 2 * KC + kc + 1)
                for m in range(2):
                    query_part(m, kc)
            key_scores(0)
            for m in range(2, 2 * PH):
                pe.wait_ge(split_lo, 28 + m + 1)
                pe.wait_ge(q_taken, m - 1)
                for kc in range(KC):
                    query_part(m, kc)
                key_scores(m - 1)
            key_scores(2 * PH - 1)

            def products(b, p, free):
                pe.wait_ge(u_lo, b + 1)
                if free is not None:
                    pe.wait_ge(gelu_done, free)
                hi = ws_hi[p][:].rearrange("p (c n) -> p c n", c=KC)
                lo = ws_lo[p][:].rearrange("p (c n) -> p c n", c=KC)
                for kc in range(KC):
                    last = split_mm(ps[:, p, :], hi[:, kc, :], lo[:, kc, :], hT_hi[:, kc, :], hT_lo[:, kc, :],
                                    kc == 0, kc == KC - 1)
                last.then_inc(act_done, 1)

            def spread(q, p, free):
                pe.wait_ge(oh_done, q + 1)
                if free is not None:
                    pe.wait_ge(w_evac, free)
                for t in range(TOK_STEP):
                    o = ps[:, 2 + 2 * p + t // 4, (t % 4) * P:(t % 4 + 1) * P]
                    for r in range(2):
                        last = pe.matmul(o, onehot[:, p, 2, t, :], onehot[:, p, r, t, :], start=r == 0, stop=r == 1)
                last.then_inc(w_mm, 1)

            for b in range(2):
                products(b, b, None)
            with pe.Fori(1, PART_A // 2) as i:
                for p in range(2):
                    products(2 * i + p, p, 2 * i + (p - 1))
            pe.wait_ge(soft_step, 3)
            for r in range(3):
                for tb in range(TB):
                    last = pe.transpose(ps[:, 2 + r, tb * P:(tb + 1) * P], picks[:, r, tb, :], ident[:])
                last.then_inc(ptr_done, 1)
            for p in range(2):
                products(PART_A + p, p, PART_A + p - 1)
                spread(p, p, None)
            with pe.Fori(1, PART_B // 2) as i:
                for p in range(2):
                    products(2 * i + (PART_A + p), p, 2 * i + (PART_A + p - 1))
                    spread(2 * i + p, p, 4 * i + (2 * p - 2))
            with pe.Fori((PART_A + PART_B) // 2, EB // 2) as i:
                for p in range(2):
                    products(2 * i + p, p, 2 * i + (p - 1))

            def mix_experts(b, p, first=False, final=False):
                pe.wait_ge(coef_l, b + 1)
                for tb in range(TB):
                    for half in range(2):
                        tok = slice(tb * P, (tb + 1) * P)
                        col = slice(half * 512, half * 512 + 512)
                        last = split_mm(ps[:, 2 * tb + half, :], coef_hi[:, p, tok], coef_lo[:, p, tok],
                                        ws_hi[p][:, col], ws_lo[p][:, col], first, final)
                    if final:
                        last.then_inc(v_whole, 1)
                if not final:
                    last.then_inc(v_mm, 1)

            pe.wait_ge(gelu_done, EB)
            mix_experts(0, 0, first=True)
            mix_experts(1, 1)
            with pe.Fori(1, EB // 2 - 1) as i:
                for p in range(2):
                    mix_experts(2 * i + p, p)
            mix_experts(EB - 2, 0)
            mix_experts(EB - 1, 1, final=True)


def tables():
    rows = N // GRID_W
    row_ids = np.repeat(np.arange(rows, dtype=np.float32), GRID_W)
    col_ids = np.tile(np.arange(GRID_W, dtype=np.float32), rows)
    pairs = DH // 4
    freqs = (np.float32(10000.0) ** (-np.arange(pairs, dtype=np.float32) / np.float32(pairs))).astype(np.float32)
    ang = np.concatenate([row_ids[:, None] * freqs, col_ids[:, None] * freqs], axis=-1).astype(np.float32)
    cos, sin = np.cos(ang).astype(np.float32), np.sin(ang).astype(np.float32)
    s = np.float32(DH ** -0.5)
    kinds = np.stack([cos, -sin, sin, cos * s, -sin * s, sin * s], axis=1)
    rope = np.ascontiguousarray(kinds.reshape(TB, P, ROPE_KINDS, 32).transpose(1, 0, 2, 3))
    t = np.arange(N)
    a = 2 * np.pi * (np.outer(t, t) % N) / N
    big = np.stack([np.cos(a), np.sin(a)]).reshape(2 * TB, P, N).transpose(1, 0, 2)
    c = np.arange(P)
    a = 2 * np.pi * (np.outer(c, c) % P) / P
    small = np.stack([np.cos(a), -np.sin(a)], axis=1) / 256.0
    f = np.float32
    return rope, np.ascontiguousarray(big.astype(f)), np.ascontiguousarray(small.astype(f)), np.eye(P, dtype=f)


def layout(x, c, ctx, c_ctx, w_ada, b_ada, norm_pre_mix, norm_post_mix, w_in, ret_decay_fwd, ret_decay_bwd,
           ret_norm_gain, w_out, norm_pre_ffn, norm_post_ffn, peer_w_query, peer_sub_keys_1, peer_sub_keys_2,
           peer_u, peer_v):
    def col(a, n):
        return np.asarray(a).reshape(n, P).T

    cc = np.stack([col(c[0], KC), col(c_ctx, KC)], axis=2).reshape(P, 2 * KC)
    dec = np.stack([np.asarray(ret_decay_fwd)[0], np.asarray(ret_decay_bwd)[0]])
    dec_pairs = np.repeat(dec.reshape(2, PAIRS, 2).transpose(2, 0, 1).reshape(2, 2 * PAIRS), DH, axis=0)
    dec_heads = np.broadcast_to(dec.reshape(1, 2 * HEADS), (P, 2 * HEADS))
    cols = np.concatenate([cc, col(b_ada[0], 6 * KC), col(norm_pre_mix[0], KC), col(norm_pre_ffn[0], KC),
                           col(norm_post_mix[0], KC), col(norm_post_ffn[0], KC), col(ret_norm_gain[0], PAIRS), dec_pairs,
                           dec_heads], axis=1)
    keys = np.stack([np.asarray(peer_sub_keys_1)[0].T, np.asarray(peer_sub_keys_2)[0].T], axis=1)
    u_t = np.asarray(peer_u)[0].reshape(EB, P, KC, P).transpose(0, 3, 2, 1).reshape(EB, P, D)
    rope, dft, dft_small, ident = tables()
    return {"x": np.asarray(x)[0], "ctxt": np.asarray(ctx)[0], "cols": cols, "w_ada": np.asarray(w_ada)[0],
            "w_in": np.asarray(w_in)[0], "w_out": np.asarray(w_out)[0],
            "w_q": np.asarray(peer_w_query)[0], "keys": keys, "u_t": u_t, "v_nat": np.asarray(peer_v)[0],
            "rope": rope, "dft": dft, "dft_small": dft_small, "ident_in": ident}


def kernel(**inputs):
    import concourse.bacc as bacc
    from concourse.bass_utils import run_bass_kernel_spmd

    nc = bacc.Bacc("TRN2", target_bir_lowering=False, num_devices=1)
    arrays = {n: np.ascontiguousarray(a) for n, a in layout(**inputs).items()}
    args = {n: nc.dram_tensor(n, list(a.shape), F32, kind="ExternalInput").ap() for n, a in arrays.items()}
    out = nc.dram_tensor("out", [N, D], F32, kind="ExternalOutput").ap()
    g_dram = nc.dram_tensor("g_dram", [P, EB * N + 1024], F32).ap()
    w_dram = nc.dram_tensor("w_dram", [N // CHUNK, P, EB * CHUNK], F32).ap()
    build(nc, **args, out=out, g_dram=g_dram, w_dram=w_dram)
    r = run_bass_kernel_spmd(nc, [arrays], core_ids=[0])
    return r.results[0]["out"].reshape(1, N, D)
```
